# Optimizing a Trainium2 kernel written in Bass

```python
import jax, jax.numpy as jnp
from jax import lax
import numpy as np

D_MODEL = 1024
BATCH = 1
SEQ = 128
DEPTH = 2
DEC_BATCH = 1
DEC_SEQ = 256
PAST_LEN = 128

GRID_W = 64
BLOCK = 128
ROPE_BASE = 10000.0
EPS = 1e-6
NEG_INF = -1e30
N_MOD = 6

POOL_WINDOWS = (2, 4, 8, 16)
POOL_GROUPS = 4
POOL_GROUP_DIM = 128
POOL_WIDTH = POOL_GROUPS * POOL_GROUP_DIM
SWA_HEADS = 8
SWA_KV_HEADS = 2
SWA_GROUP = SWA_HEADS // SWA_KV_HEADS
SWA_HEAD_DIM = 64
SWA_WINDOW = 128
MLA_HEADS = 8
MLA_Q_RANK = 384
MLA_KV_RANK = 256
MLA_NOPE_DIM = 64
MLA_ROPE_DIM = 32
MLA_QK_DIM = MLA_NOPE_DIM + MLA_ROPE_DIM
MLA_V_DIM = 64
N_BRANCHES = 3
BRANCH_A_WIDTH = POOL_WIDTH
BRANCH_B_WIDTH = SWA_HEADS * SWA_HEAD_DIM
BRANCH_C_WIDTH = MLA_HEADS * MLA_V_DIM
IN_WIDTHS = (POOL_WIDTH, SWA_HEADS * SWA_HEAD_DIM, SWA_KV_HEADS * SWA_HEAD_DIM,
             SWA_KV_HEADS * SWA_HEAD_DIM, MLA_Q_RANK, MLA_KV_RANK, MLA_ROPE_DIM,
             N_BRANCHES * D_MODEL)
IN_WIDTH = sum(IN_WIDTHS)
N_EXPERTS = 16
EXPERT_HIDDEN = 1024
CAPACITY_FACTOR = 2

kernel_name = 'hybrid_dit_pool_swa_mla_ec'

def rmsnorm(x, g):
    xf = x.astype(jnp.float32)
    y = xf * lax.rsqrt(jnp.mean(xf * xf, axis=-1, keepdims=True) + EPS)
    return (y * g.astype(jnp.float32)).astype(x.dtype)

def split_in(z):
    outs, off = [], 0
    for w in IN_WIDTHS:
        outs.append(z[..., off:off + w])
        off += w
    return outs

def grid_positions(n):
    rows = n // GRID_W
    row = jnp.repeat(jnp.arange(rows), GRID_W)
    col = jnp.tile(jnp.arange(GRID_W), rows)
    return row, col

def rope_1d(x, pos):
    half = x.shape[-1] // 2
    freqs = ROPE_BASE ** (-jnp.arange(half, dtype=jnp.float32) / half)
    ang = pos.astype(jnp.float32)[:, None] * freqs[None, :]
    cos = jnp.cos(ang)[None, :, None, :]
    sin = jnp.sin(ang)[None, :, None, :]
    xf = x.astype(jnp.float32)
    x1, x2 = xf[..., :half], xf[..., half:]
    return jnp.concatenate([x1 * cos - x2 * sin, x1 * sin + x2 * cos], axis=-1).astype(x.dtype)

def rope_2d(x):
    row, col = grid_positions(x.shape[1])
    h = x.shape[-1] // 2
    return jnp.concatenate([rope_1d(x[..., :h], row), rope_1d(x[..., h:], col)], axis=-1)

def rope_mla(x):
    return jnp.concatenate([x[..., :MLA_NOPE_DIM], rope_2d(x[..., MLA_NOPE_DIM:])], axis=-1)

def pool_mixer(u, w_pool, pool_scale):
    n = u.shape[1]
    uf = u.astype(jnp.float32)
    cs = jnp.concatenate([jnp.zeros_like(uf[:, :1]), jnp.cumsum(uf, axis=1)], axis=1)
    t = jnp.arange(n)
    outs = []
    for g, w in enumerate(POOL_WINDOWS):
        sl = slice(g * POOL_GROUP_DIM, (g + 1) * POOL_GROUP_DIM)
        lo = jnp.clip(t - w // 2, 0, n)
        hi = jnp.clip(t + w // 2, 0, n)
        cnt = (hi - lo).astype(jnp.float32)[None, :, None]
        mean = (cs[:, hi, sl] - cs[:, lo, sl]) / cnt
        outs.append(jnp.einsum('bnc,cd->bnd', (mean - uf[..., sl]).astype(u.dtype), w_pool[g]))
    return jnp.concatenate(outs, axis=-1) * pool_scale

def dense_attn(q, k, v, sink=None):
    b, n, kvh, g, d = q.shape
    nb = n // BLOCK
    qb = jnp.moveaxis(q.reshape(b, nb, BLOCK, kvh, g, d), 1, 0)
    scale = d ** -0.5

    def one(qblk):
        s = jnp.einsum('bqhgd,bkhd->bhgqk', qblk, k).astype(jnp.float32) * scale
        if sink is None:
            p = jax.nn.softmax(s, axis=-1)
        else:
            sk = jnp.broadcast_to(sink.astype(jnp.float32)[None, :, :, None, None], s.shape[:-1] + (1,))
            p = jax.nn.softmax(jnp.concatenate([s, sk], axis=-1), axis=-1)[..., :-1]
        return jnp.einsum('bhgqk,bkhd->bqhgd', p.astype(v.dtype), v)

    o = lax.map(one, qb)
    return jnp.moveaxis(o, 0, 1).reshape(b, n, kvh * g * v.shape[-1])

def banded_attn(q, k, v, k_ctx, v_ctx, sink):
    b, n, kvh, g, d = q.shape
    nb = n // BLOCK
    qb = q.reshape(b, nb, BLOCK, kvh, g, d)

    def band(x):
        xp = jnp.pad(x, ((0, 0), (BLOCK, BLOCK), (0, 0), (0, 0))).reshape(b, nb + 2, BLOCK, kvh, x.shape[-1])
        return jnp.concatenate([xp[:, :-2], xp[:, 1:-1], xp[:, 2:]], axis=2)

    kw, vw = band(k), band(v)
    qpos = jnp.arange(nb)[:, None] * BLOCK + jnp.arange(BLOCK)[None, :]
    kpos = (jnp.arange(nb)[:, None] - 1) * BLOCK + jnp.arange(3 * BLOCK)[None, :]
    kp = kpos[:, None, :]
    mask = (jnp.abs(kp - qpos[:, :, None]) <= SWA_WINDOW) & (kp >= 0) & (kp < n)
    scale = d ** -0.5
    s_loc = jnp.einsum('bnqhgd,bnkhd->bhgnqk', qb, kw).astype(jnp.float32) * scale
    s_loc = jnp.where(mask, s_loc, NEG_INF)
    s_ctx = jnp.einsum('bnqhgd,bkhd->bhgnqk', qb, k_ctx).astype(jnp.float32) * scale
    sk = jnp.broadcast_to(sink.astype(jnp.float32)[None, :, :, None, None, None], s_loc.shape[:-1] + (1,))
    p = jax.nn.softmax(jnp.concatenate([s_loc, s_ctx, sk], axis=-1), axis=-1)
    wl = 3 * BLOCK
    p_loc = p[..., :wl].astype(v.dtype)
    p_ctx = p[..., wl:-1].astype(v.dtype)
    o = (jnp.einsum('bhgnqk,bnkhd->bnqhgd', p_loc, vw)
         + jnp.einsum('bhgnqk,bkhd->bnqhgd', p_ctx, v_ctx))
    return o.reshape(b, n, kvh * g * v.shape[-1])

def mla_kv(ckv, krope, w_kv_b, k_g):
    b, m, _ = ckv.shape
    kv = jnp.einsum('bmr,rf->bmf', ckv, w_kv_b).reshape(b, m, MLA_HEADS, MLA_NOPE_DIM + MLA_V_DIM)
    kr = jnp.broadcast_to(krope[:, :, None, :], (b, m, MLA_HEADS, MLA_ROPE_DIM))
    k = rmsnorm(jnp.concatenate([kv[..., :MLA_NOPE_DIM], kr], axis=-1), k_g)
    return k, kv[..., MLA_NOPE_DIM:]

def token_mixing(h, lp, ctx=None):
    b, n, _ = h.shape
    z = jnp.einsum('bnd,df->bnf', h, lp['w_in'])
    u_a, q_b, k_b, v_b, q_c, kv_c, kr_c, gts = split_in(z)
    ya = pool_mixer(u_a, lp['pool_w'], lp['pool_scale'])
    qs = rmsnorm(q_b.reshape(b, n, SWA_HEADS, SWA_HEAD_DIM), lp['swa_q_g'])
    ks = rmsnorm(k_b.reshape(b, n, SWA_KV_HEADS, SWA_HEAD_DIM), lp['swa_k_g'])
    vs = v_b.reshape(b, n, SWA_KV_HEADS, SWA_HEAD_DIM)
    sink = lp['sink'].reshape(SWA_KV_HEADS, SWA_GROUP)
    ckv = rmsnorm(kv_c, lp['mla_kv_norm_g'])
    qm = jnp.einsum('bnr,rf->bnf', rmsnorm(q_c, lp['mla_q_norm_g']), lp['w_q_b'])
    qm = rmsnorm(qm.reshape(b, n, MLA_HEADS, MLA_QK_DIM), lp['mla_q_g'])
    km, vm = mla_kv(ckv, kr_c, lp['w_kv_b'], lp['mla_k_g'])
    if ctx is None:
        yb = dense_attn(qs.reshape(b, n, SWA_KV_HEADS, SWA_GROUP, SWA_HEAD_DIM), ks, vs, sink)
        yc = dense_attn(qm[:, :, :, None, :], km, vm)
        new = (ks, vs, ckv, kr_c)
    else:
        ck, cv, cckv, ckr = ctx
        qs, ks = rope_2d(qs), rope_2d(ks)
        yb = banded_attn(qs.reshape(b, n, SWA_KV_HEADS, SWA_GROUP, SWA_HEAD_DIM), ks, vs, ck, cv, sink)
        qm, km = rope_mla(qm), rope_mla(km)
        kmc, vmc = mla_kv(cckv, ckr, lp['w_kv_b'], lp['mla_k_g'])
        yc = dense_attn(qm[:, :, :, None, :], jnp.concatenate([km, kmc], axis=1),
                        jnp.concatenate([vm, vmc], axis=1))
        new = None
    gate = jax.nn.sigmoid(gts.astype(jnp.float32)).astype(h.dtype).reshape(b, n, N_BRANCHES, D_MODEL)
    merged = (gate[:, :, 0] * jnp.einsum('bnc,cd->bnd', ya, lp['w_br_a'])
              + gate[:, :, 1] * jnp.einsum('bnc,cd->bnd', yb, lp['w_br_b'])
              + gate[:, :, 2] * jnp.einsum('bnc,cd->bnd', yc, lp['w_br_c']))
    return jnp.einsum('bnd,de->bne', merged, lp['w_out']), new

def ec_moe(h, w_router, w_gate, w_up, w_down):
    b, n, d = h.shape
    cap = CAPACITY_FACTOR * n // N_EXPERTS
    aff = jax.nn.softmax(jnp.einsum('bnd,de->ben', h, w_router).astype(jnp.float32), axis=1)
    vals, idx = lax.top_k(aff, cap)
    xg = jax.vmap(lambda hb, ib: hb[ib])(h, idx)
    a = jnp.einsum('becd,edf->becf', xg, w_gate)
    u = jnp.einsum('becd,edf->becf', xg, w_up)
    o = jnp.einsum('becf,efd->becd', jax.nn.silu(a) * u, w_down) * vals[..., None].astype(h.dtype)
    return jax.vmap(lambda ib, ob: jnp.zeros((n, d), ob.dtype).at[ib.reshape(-1)].add(ob.reshape(-1, d)))(idx, o)

def block(x, mod, lp, ctx=None):
    sh1, sc1, g1, sh2, sc2, g2 = jnp.split(mod, N_MOD, axis=-1)
    h = rmsnorm(x, lp['norm1_g']) * (1 + sc1) + sh1
    y, new = token_mixing(h, lp, ctx)
    x = x + g1 * y
    h = rmsnorm(x, lp['norm2_g']) * (1 + sc2) + sh2
    x = x + g2 * ec_moe(h, lp['w_router'], lp['w_gate'], lp['w_up'], lp['w_down'])
    return x, new

def setup_inputs(seed: int = 0) -> dict:
    key = jax.random.key(seed)
    ks = jax.random.split(key, 40)
    f32 = jnp.float32

    def nrm(i, shape, scale=1.0):
        return jax.random.normal(ks[i], shape, f32) * scale

    L = DEPTH
    return {
        'x_prompt': nrm(0, (BATCH, SEQ, D_MODEL)),
        'x_sample': nrm(1, (DEC_BATCH, DEC_SEQ, D_MODEL)),
        'cache_swa_k': nrm(2, (DEC_BATCH, L, PAST_LEN, SWA_KV_HEADS, SWA_HEAD_DIM)),
        'cache_swa_v': nrm(3, (DEC_BATCH, L, PAST_LEN, SWA_KV_HEADS, SWA_HEAD_DIM)),
        'cache_mla_ckv': nrm(4, (DEC_BATCH, L, PAST_LEN, MLA_KV_RANK)),
        'cache_mla_krope': nrm(5, (DEC_BATCH, L, PAST_LEN, MLA_ROPE_DIM)),
        'c': nrm(6, (DEC_BATCH, D_MODEL)),
        'c_ctx': nrm(7, (D_MODEL,)),
        'w_mod': nrm(8, (L, D_MODEL, N_MOD * D_MODEL), 0.5 * D_MODEL ** -0.5),
        'b_mod': nrm(9, (L, N_MOD * D_MODEL), 0.1),
        'norm1_g': 1.0 + nrm(10, (L, D_MODEL), 0.1),
        'norm2_g': 1.0 + nrm(11, (L, D_MODEL), 0.1),
        'w_in': nrm(12, (L, D_MODEL, IN_WIDTH), D_MODEL ** -0.5),
        'pool_w': nrm(13, (L, POOL_GROUPS, POOL_GROUP_DIM, POOL_GROUP_DIM), POOL_GROUP_DIM ** -0.5),
        'pool_scale': 1.0 + nrm(14, (L, POOL_WIDTH), 0.1),
        'swa_q_g': 1.0 + nrm(15, (L, SWA_HEAD_DIM), 0.1),
        'swa_k_g': 1.0 + nrm(16, (L, SWA_HEAD_DIM), 0.1),
        'sink': nrm(17, (L, SWA_HEADS), 0.5),
        'mla_q_norm_g': 1.0 + nrm(18, (L, MLA_Q_RANK), 0.1),
        'w_q_b': nrm(19, (L, MLA_Q_RANK, MLA_HEADS * MLA_QK_DIM), MLA_Q_RANK ** -0.5),
        'mla_kv_norm_g': 1.0 + nrm(20, (L, MLA_KV_RANK), 0.1),
        'w_kv_b': nrm(21, (L, MLA_KV_RANK, MLA_HEADS * (MLA_NOPE_DIM + MLA_V_DIM)), MLA_KV_RANK ** -0.5),
        'mla_q_g': 1.0 + nrm(22, (L, MLA_QK_DIM), 0.1),
        'mla_k_g': 1.0 + nrm(23, (L, MLA_QK_DIM), 0.1),
        'w_br_a': nrm(24, (L, BRANCH_A_WIDTH, D_MODEL), BRANCH_A_WIDTH ** -0.5),
        'w_br_b': nrm(25, (L, BRANCH_B_WIDTH, D_MODEL), BRANCH_B_WIDTH ** -0.5),
        'w_br_c': nrm(26, (L, BRANCH_C_WIDTH, D_MODEL), BRANCH_C_WIDTH ** -0.5),
        'w_out': nrm(27, (L, D_MODEL, D_MODEL), D_MODEL ** -0.5),
        'w_router': nrm(28, (L, D_MODEL, N_EXPERTS), D_MODEL ** -0.5),
        'w_gate': nrm(29, (L, N_EXPERTS, D_MODEL, EXPERT_HIDDEN), D_MODEL ** -0.5),
        'w_up': nrm(30, (L, N_EXPERTS, D_MODEL, EXPERT_HIDDEN), D_MODEL ** -0.5),
        'w_down': nrm(31, (L, N_EXPERTS, EXPERT_HIDDEN, D_MODEL), EXPERT_HIDDEN ** -0.5),
    }

def reference(x_prompt, x_sample, cache_swa_k, cache_swa_v, cache_mla_ckv, cache_mla_krope,
              c, c_ctx, w_mod, b_mod, norm1_g, norm2_g, w_in, pool_w, pool_scale,
              swa_q_g, swa_k_g, sink, mla_q_norm_g, w_q_b, mla_kv_norm_g, w_kv_b,
              mla_q_g, mla_k_g, w_br_a, w_br_b, w_br_c, w_out,
              w_router, w_gate, w_up, w_down):
    xp, xs = x_prompt, x_sample
    new_k, new_v, new_ckv, new_kr = [], [], [], []
    for l in range(DEPTH):
        lp = {
            'norm1_g': norm1_g[l], 'norm2_g': norm2_g[l], 'w_in': w_in[l],
            'pool_w': pool_w[l], 'pool_scale': pool_scale[l],
            'swa_q_g': swa_q_g[l], 'swa_k_g': swa_k_g[l], 'sink': sink[l],
            'mla_q_norm_g': mla_q_norm_g[l], 'w_q_b': w_q_b[l],
            'mla_kv_norm_g': mla_kv_norm_g[l], 'w_kv_b': w_kv_b[l],
            'mla_q_g': mla_q_g[l], 'mla_k_g': mla_k_g[l],
            'w_br_a': w_br_a[l], 'w_br_b': w_br_b[l], 'w_br_c': w_br_c[l], 'w_out': w_out[l],
            'w_router': w_router[l], 'w_gate': w_gate[l], 'w_up': w_up[l], 'w_down': w_down[l],
        }
        mod_ctx = (jax.nn.silu(c_ctx) @ w_mod[l] + b_mod[l])[None, None, :]
        xp, (k_l, v_l, ckv_l, kr_l) = block(xp, mod_ctx, lp)
        new_k.append(k_l)
        new_v.append(v_l)
        new_ckv.append(ckv_l)
        new_kr.append(kr_l)
        mod_lat = (jax.nn.silu(c) @ w_mod[l] + b_mod[l])[:, None, :]
        xs, _ = block(xs, mod_lat, lp,
                      (cache_swa_k[:, l], cache_swa_v[:, l], cache_mla_ckv[:, l], cache_mla_krope[:, l]))
    new_swa_k = jnp.stack(new_k, axis=1)
    new_swa_v = jnp.stack(new_v, axis=1)
    new_mla_ckv = jnp.stack(new_ckv, axis=1)
    new_mla_krope = jnp.stack(new_kr, axis=1)
    return (xp, xs, new_swa_k, new_swa_v, new_mla_ckv, new_mla_krope)


_drawn_inputs = setup_inputs


def setup_inputs(seed=0):
    import zlib

    import numpy as np

    out = dict(_drawn_inputs(seed))
    spreads = {}
    factors = {'cache_swa_k': 4.308,
     'cache_swa_v': 3.605,
     'cache_mla_ckv': 4.3,
     'cache_mla_krope': 6.784,
     'swa_q_g': 8.0,
     'sink': 64.0,
     'mla_q_norm_g': 8.0,
     'mla_q_g': 8.0,
     'mla_k_g': 8.0}
    for name, (base, spread) in spreads.items():
        noise = np.random.default_rng([zlib.crc32(name.encode()), seed]).standard_normal(out[name].shape)
        drawn = base * np.exp(spread * noise) if base else spread * noise
        out[name] = __import__('jax').numpy.asarray(drawn.astype(out[name].dtype))
    for name, factor in factors.items():
        out[name] = (out[name] * factor).astype(out[name].dtype)
    return out
```

```python
from contextlib import ExitStack

import numpy as np

import concourse.bass as bass
from concourse import mybir

F32 = mybir.dt.float32
ALU = mybir.AluOpType
ACT = mybir.ActivationFunctionType
AX = mybir.AxisListType.X

P = 128
D = 1024
KB = D // P
L = 2
T = 3
TOK = T * P
EPS = 1e-6
SH, SD = 8, 64
MH, MQ, NOPE, ROPE, MV = 8, 96, 64, 32, 64
QR, KVR = 384, 256
NE = 16
CP, CS = 16, 32
SLOTS = 64
USED = CP + CS
NP = NE // 2
UNIT = 2048
RING = 8
NEG = -1e30
BIG = 4096.0

COL_B, COL_N1, COL_N2, COL_PS, NCOL = 0, 48, 56, 64, 68
ROW_QG, ROW_KG, ROW_QCG, ROW_KVG, ROW_MQG, ROW_MKG, ROW_SINK, NROW = 0, 64, 128, 512, 768, 864, 960, 968
_sizes = [("ident", P), ("tri", P), ("ones", P), ("pick0", P), ("pick1", P), ("pickslot", P), ("pair", 2),
          ("slotno", 2 * SLOTS), ("band", 2 * P), ("ropes", 2 * 2 * SD), ("ropem", 2 * 2 * ROPE)]
CONST = {}
_at = 0
for _n, _s in _sizes:
    CONST[_n] = (_at, _at + _s)
    _at += _s
NCONST = _at


def const_table():
    t = np.zeros((P, NCONST), np.float32)
    r = np.arange(P)

    def put(name, a):
        lo, hi = CONST[name]
        t[:, lo:hi] = a.reshape(P, hi - lo)
    put("ident", np.eye(P))
    put("tri", (r[:, None] < r[None, :]).astype(np.float32))
    put("ones", np.ones((P, P)))
    put("pick0", np.repeat((r % 32 == 0)[:, None], P, 1))
    put("pick1", np.repeat((r % 32 == 1)[:, None], P, 1))
    s = r % SLOTS
    stream = np.where(s < CP, 0, np.where(s < USED, 1, -1))
    put("pickslot", (r[:, None] % 32 == stream[None, :]))
    put("pair", np.stack([r % 32 == 0, r % 32 == 1], 1))
    k = np.arange(SLOTS)
    put("slotno", np.repeat(np.stack([np.where(k < CP, k, -1), np.where((k >= CP) & (k < USED), k - CP, -1)])[None], P, 0))
    put("band", np.stack([np.where(r[None, :] <= r[:, None], 0, NEG), np.where(r[:, None] <= r[None, :], 0, NEG)], 1))

    def rope(width):
        q = width // 4
        f = (np.float32(10000.0) ** (-np.arange(q, dtype=np.float32) / np.float32(q))).astype(np.float32)
        pos = np.arange(2 * P)
        out = np.zeros((P, 2, 2, 2, 2, q), np.float32)
        for axis, where in enumerate((pos // 64, pos % 64)):
            ang = (where.astype(np.float32)[:, None] * f[None, :]).astype(np.float32).astype(np.float64)
            c, s = (g(ang).reshape(2, P, q).transpose(1, 0, 2) for g in (np.cos, np.sin))
            out[:, :, 0, axis, 0] = out[:, :, 0, axis, 1] = c
            out[:, :, 1, axis, 0], out[:, :, 1, axis, 1] = -s, s
        return out
    put("ropes", rope(SD))
    put("ropem", rope(ROPE))
    return t


PADW = 416
PSEG = ((8, 0, P), (8 + P + 8 + 8, P, 2 * P))


def count_table():
    out = np.zeros((4, TOK), np.float32)
    for g in range(4):
        w = 2 << g
        for _, t0, n in PSEG:
            t = np.arange(n)
            out[g, t0:t0 + n] = 1.0 / (np.clip(t + w // 2, 0, n) - np.clip(t - w // 2, 0, n))
    return out.reshape(1, 4 * TOK)


def plan_banks():
    uses = []

    def use(name, bank):
        uses.append((name, bank))
    for i in range(4):
        use(("mod", i), i % 2)
    use(("modcol", 0), 2)
    for kb in range(KB):
        use(("h1", kb), 4 + kb % 4)
    for s in range(3):
        for t in range(T):
            use(("seg", s, t), (3 * s + t) % 8)
    for g in range(4):
        use(("u", g), 1 + g)
    for t in range(T):
        use(("tq", t), 5 + t)
    for t in range(T):
        use(("tkc", t), t)
    for t in range(2):
        use(("tkv", t), 3 + t)
    for h in range(2):
        for t in range(T):
            use(("wq", h, t), 1 + 3 * h + t)
    for g in range(4):
        use(("pool", g), (7, 0)[g % 2])
    for t in range(4):
        for h in range(2):
            use(("wkv", t, h), (1, 3, 5, 1)[t] + h)
        if t < 3:
            for h in range(2):
                use(("tqm", t, h), (7, 0)[h])
    for t in range(4):
        for h in range(2):
            use(("tkm", t, h), (3 + 2 * t + h) % 8 if t < 3 else 1 + h)
    for i in range(SH + MH):
        use(("sa", i), 2 * (i % 2))
        use(("sb", i), 2 * (i % 2) + 1)
        use(("x", i), 4)
        use(("y", i), 5)
        if i % 2 == 0:
            use(("o", i // 2), 6)
        use(("gate", i // 8, i % 8), 7)
        use(("br", i // 8, i % 8), 7)
    for i in (4, 5):
        use(("mod", i), i - 1)
    for i in (4, 5):
        for v in range(2):
            use(("modb", i, v), 5 + v)
    for j in range(KB):
        use(("gate", 2, j), (7, 0)[j % 2])
        use(("br", 2, j), (1, 2)[j % 2])
    for n in range(2):
        for t in range(T):
            use(("wo", n, t), 3 * n + t)
    for i in range(6, 12):
        use(("mod", i), 6 + i % 2)
    use(("modcol", 1), 0)
    for i in (10, 11):
        use(("modb", i, 0), i - 9)
    for kb in range(KB):
        use(("h2", kb), 2 + kb % 4)
    use(("route", 0), 6)
    use(("afft", 0), 7)
    use(("get", 0), 0)
    use(("cum", 0), 1)
    for p in range(NP):
        use(("selt", p), 2 + p % 4)
    for kb in range(KB):
        for h in range(2):
            use(("gather", kb, h), (6, 7, 0, 1)[(2 * kb + h) % 4])
    count, where = [0] * 8, {}
    for name, bank in uses:
        where[name] = (bank, count[bank])
        count[bank] += 1
    return where, count


WHERE, MIXED = plan_banks()
BANK_G, BANK_U, BANK_D, BANK_T, BANK_Y = (0, 2), (1, 3), (5, 6), 4, 7
PAIR = [1, 1, 1, 1, 5, 1, 1, 3]
BANKS = [m + NP * k for m, k in zip(MIXED, PAIR)]


def plan_units():
    units = []
    for i in range(4):
        units += [("mod", i, 0), ("mod", i, 1)]
    for s in range(4):
        units += [("seg", s, 0), ("seg", s, 1)]
    units += [("wq", 0, 0), ("wq", 1, 0), ("wkv", 0, 0)]
    for b in range(3):
        if b == 2:
            for i in (4, 5):
                units += [("mod", i, 0), ("mod", i, 1)]
        for h in range(2):
            units += [("gate", (b, h), 0), ("gate", (b, h), 1), ("br", (b, h), 0)]
    for n in range(2):
        units += [("wo", n, 0), ("wo", n, 1)]
    for i in range(6, 12):
        units += [("mod", i, 0), ("mod", i, 1)]
    return units


UNITS = plan_units()
NU = len(UNITS)
MIX_ROUNDS = -(-NU // RING)
UNIT_AT = {u: n for n, u in enumerate(UNITS)}
LANDED = [sum(n % RING == s for n in range(NU)) for s in range(RING)]
LANDS = [c + 3 * NP for c in LANDED]
FIRSTS = [u for u in UNITS if u[2] == 0 and u[0] in ("mod", "seg", "gate", "wo")]
FIRST_AT = {u: n for n, u in enumerate(FIRSTS)}
HALVES = len(FIRSTS) + 12 * NP


def last_group(u):
    kind, i, _ = u
    if kind == "mod":
        return ("mod", i)
    if kind == "seg":
        return ("seg", i, 2) if i < 3 else ("u", 3)
    if kind == "wq":
        return ("wq", i, 2)
    if kind == "wkv":
        return ("wkv", 3, 1)
    if kind in ("gate", "br"):
        return (kind, i[0], 4 * i[1] + 3)
    return ("wo", i, 2)


def hybrid_step(nc, a, outs):
    with ExitStack() as ctx:
        def sb(name, shape):
            return ctx.enter_context(nc.sbuf_tensor(name, shape, F32))

        def sem(name):
            return ctx.enter_context(nc.semaphore(name))

        x = sb("x", [P, T, D])
        hT = sb("hT", [P, KB, TOK])
        xn = sb("xn", [P, T, D])
        merged = xn[:, :, :].rearrange("p t d -> p (t d)").rearrange("p (k n) -> p k n", n=TOK)
        ring = sb("ring", [P, RING, UNIT])
        kTp = sb("kTp", [P, 2, 512])
        xcur = sb("xcur", [P, 2, KB, SLOTS])
        cols = sb("cols", [P, L, NCOL])
        rows = sb("rows", [P, NROW])
        const = sb("const", [P, NCONST])
        cs = sb("cs", [P, KB, 32])
        modrow = sb("modrow", [P, 2, 512])
        shift = sb("shift", [P, KB, 2])
        amp = sb("amp", [P, KB, 2])
        g2slot = sb("g2slot", [P, D])
        wrout = sb("wrout", [P, KB, NE])
        kr = sb("kr", [P, 4, ROPE])
        krg = sb("krg", [P, 4, ROPE])
        sskr = sb("sskr", [P, 4])
        ss = sb("ss", [P, 98])
        var = sb("var", [P, 98])
        rstd = sb("rstd", [P, 98])
        mhalf = sb("mhalf", [P, 8])
        negsink = sb("negsink", [P, SH])
        mx = sb("mx", [P, 2, 3])
        negm = sb("negm", [P, 2, 3])
        rsum = sb("rsum", [P, 2, 3])
        esink = sb("esink", [P, 2, 3])
        rinv = sb("rinv", [P, 2, 3])

        M = sb("M", [P, 19584])

        def view(at, *dims):
            n = int(np.prod(dims))
            v = M[:, at:at + n]
            if len(dims) == 2:
                v = v.rearrange("p (a b) -> p a b", b=dims[1])
            if len(dims) == 3:
                v = v.rearrange("p (a b c) -> p a b c", b=dims[1], c=dims[2])
            return v
        qmT = view(0, MH, TOK)
        upad = view(0, 4, PADW)
        win = view(4 * PADW, 2, PADW)
        kmT = view(3072, MH, 512)
        qtok = view(3072, T, 512)
        ktok = view(4608, T, P)
        qctok = view(4992, T, QR)
        ckvtok = view(6144, T, KVR)
        g1b = view(3072, 2, D)
        gb = view(5120, D)
        vm = view(7168, 4, MH, MV)
        inv = view(7168, 4, TOK)
        poolw = view(8704, 4, P)
        vtok = view(9216, 4, P)
        yaT = view(9728, 4, TOK)
        ybT = view(11264, 4, TOK)
        ropea = view(11264, 768)
        ropeb = view(12032, 768)
        qT = view(12800, 4, TOK)
        junk = view(14336, D)
        qcT = view(14336, 3, TOK)
        ckvT = view(15488, 2, 512)
        sqb = view(16512, 2, 768)
        tok = view(18048, 2, 768)
        cond = view(18048, KB, 32)
        prob = view(14336, 2, 896)
        probT = view(16128, 2, 7, P)
        tanh_g = view(17920, 2, TOK)
        gated = view(18688, TOK)
        wtmp = view(15360, 2, 512)
        xg = view(0, KB, NE, USED)
        selT = view(6144, NP, TOK)
        sel = view(9216, T, NE * SLOTS)
        selcur = view(12288, TOK)
        th = (view(12672, 512), view(18672, 512))
        s1 = view(13184, 512)
        hid = view(13696, 2, 512)
        hidT = view(14720, KB, P)
        osb = view(15744, D)
        gb2 = view(16768, D)
        logit = view(17792, T, NE)
        aff = view(17840, T, NE)
        small = view(17888, 16)
        affT = view(17904, TOK)
        work = view(18288, TOK)
        ge = view(18672, 2 * TOK)
        get = view(19440, T, 2 * NE)
        top8 = view(19536, 8)
        sl1 = view(17904, T, NE)
        sl2 = view(17952, T, NE)

        bank = [ctx.enter_context(nc.psum_tensor(f"bank{b}", [P, 512], F32)) for b in range(8)]

        def cst_(name, *dims):
            lo, hi = CONST[name]
            v = const[:, lo:hi]
            if len(dims) == 2:
                v = v.rearrange("p (a b) -> p a b", b=dims[1])
            if len(dims) == 3:
                v = v.rearrange("p (a b c) -> p a b c", b=dims[1], c=dims[2])
            return v
        ident, tri, ones = cst_("ident"), cst_("tri"), cst_("ones")
        pick = (cst_("pick0"), cst_("pick1"))
        pickslot, pair = cst_("pickslot"), cst_("pair")
        slotno = cst_("slotno", 2, SLOTS)
        band = cst_("band", 2, P)
        ropes = cst_("ropes", 2, 2, SD)
        ropem = cst_("ropem", 2, 2, ROPE)

        bank_full = [sem(f"bank_full{b}") for b in range(8)]
        bank_read = [sem(f"bank_read{b}") for b in range(8)]
        landed = [sem(f"landed{s}") for s in range(RING)]
        first_half_used = sem("first_half_used")
        x_in = sem("x_in")
        const_in = sem("const_in")
        layer_in = sem("layer_in")
        gate_row_in = sem("gate_row_in")
        out_done = sem("out_done")
        cache_out = sem("cache_out")
        pads_zero = sem("pads_zero")
        cond_tanh = sem("cond_tanh")
        cond_ready = sem("cond_ready")
        act_step = sem("act_step")
        dve_step = sem("dve_step")
        pool_step = sem("pool_step")
        xss_ready = sem("xss_ready")
        var_ready = sem("var_ready")
        rstd_ready = sem("rstd_ready")
        xn_ready = sem("xn_ready")
        cols_ready = sem("cols_ready")
        sq_ready = sem("sq_ready")
        sq_used = sem("sq_used")
        cseg_read = sem("cseg_read")
        dseg_read = sem("dseg_read")
        v_read = sem("v_read")
        qtok_ready = sem("qtok_ready")
        ktok_ready = sem("ktok_ready")
        qctok_ready = sem("qctok_ready")
        ckvtok_ready = sem("ckvtok_ready")
        tok_ready = sem("tok_ready")
        pool_ready = sem("pool_ready")
        negm_ready = sem("negm_ready")
        sink_ready = sem("sink_ready")
        prob_ready = sem("prob_ready")
        merged_ready = sem("merged_ready")
        x_mixed = sem("x_mixed")
        exp_in_ready = sem("exp_in_ready")
        exp_ready = sem("exp_ready")
        aff_ready = sem("aff_ready")
        ge_ready = sem("ge_ready")
        sel_ready = sem("sel_ready")
        selv_ready = sem("selv_ready")
        xcur_ready = sem("xcur_ready")
        selcur_ready = sem("selcur_ready")
        th_ready = sem("th_ready")
        s1_ready = sem("s1_ready")
        hid_ready = sem("hid_ready")

        block = ctx.enter_context(nc.Block())

        def turn(l, name):
            b, n = WHERE[name]
            return b, l * BANKS[b] + n

        def wait_full(e, l, name):
            b, n = turn(l, name)
            e.wait_ge(bank_full[b], n + 1)
            return bank[b]

        def wait_read(e, l, name):
            b, n = turn(l, name)
            e.wait_ge(bank_read[b], n + 1)

        def read(l, name, ins):
            b, _ = turn(l, name)
            ins.then_inc(bank_read[b], 1)

        def x_final(e, l):
            for b in (BANK_T, BANK_Y):
                e.wait_ge(bank_read[b], (l + 1) * BANKS[b])

        def steps(e, s):
            count = [0]

            def step(ins):
                count[0] += 1
                ins.then_inc(s, 1)
                e.wait_ge(s, count[0])
            return step

        def unit_source(l, u):
            kind, i, h = u
            if kind == "mod":
                w = a["w_mod"][l, h * 512:(h + 1) * 512, i * 512:(i + 1) * 512]
            elif kind == "seg":
                c0, n = ((512, 512), (1024, 512), (1536, 416), (0, 512))[i]
                w = a["w_in"][l, h * 512:(h + 1) * 512, c0:c0 + n]
            elif kind == "wq":
                w = a["w_q_b"][l, :, i * QR:(i + 1) * QR]
            elif kind == "wkv":
                w = a["w_kv_b"][l]
            elif kind == "gate":
                c0 = 1952 + i[0] * D + i[1] * 512
                w = a["w_in"][l, h * 512:(h + 1) * 512, c0:c0 + 512]
            elif kind == "br":
                w = a[("w_br_a", "w_br_b", "w_br_c")[i[0]]][l, :, i[1] * 512:(i[1] + 1) * 512]
            else:
                w = a["w_out"][l, h * 512:(h + 1) * 512, i * 512:(i + 1) * 512]
            return w.rearrange("(k p) n -> p k n", p=P)

        def slot_of(u):
            return UNIT_AT[u] % RING

        def unit_view(u, width=512):
            return ring[:, slot_of(u), :].rearrange("p (k n) -> p k n", n=width)

        @block.sync
        def _(sp):
            sp.dma_start(cond, a["condT"]).then_inc(const_in, 16)
            sp.dma_start(const[:, :], a["const"]).then_inc(const_in, 16)
            sp.dma_start(cols[:, :, :], a["cols"]).then_inc(const_in, 16)
            sp.dma_start(x[:, 0, :], a["x_prompt"][0]).then_inc(x_in, 16)
            sp.dma_start(x[:, 1:3, :], a["x_sample"][0].rearrange("(t p) d -> p t d", p=P)).then_inc(x_in, 16)

            def wait_pair(l, pr, j):
                g, r = j // 4, j % 4
                if r < 2:
                    sp.wait_ge(first_half_used, l * HALVES + len(FIRSTS) + pr * 12 + 2 * g + r + 1)
                else:
                    b = (0, 1, 2, 3, 5, 6)[g]
                    sp.wait_ge(bank_full[b], l * BANKS[b] + MIXED[b] + pr + 1)

            def wait_mixing(l, u):
                if u in FIRST_AT:
                    sp.wait_ge(first_half_used, l * HALVES + FIRST_AT[u] + 1)
                else:
                    wait_full(sp, l, last_group(u))

            def load_pair(l, pr, first):
                for j in range(24):
                    s = j % RING
                    if j >= RING:
                        wait_pair(l, pr, j - RING)
                    elif not first:
                        wait_pair(l, pr - 1, j + 16)
                    else:
                        before = [n for n in range(NU) if n % RING == s][-1]
                        wait_mixing(l, UNITS[before])
                    g, h, e = j // 4, (j % 4) // 2, j % 2
                    w = (a["w_gate"], a["w_up"], a["w_gate"], a["w_up"], a["w_down"], a["w_down"])[g]
                    c = (0, 0, 1, 1, 0, 1)[g]
                    src = w[l, 2 * pr + e, h * 512:(h + 1) * 512, c * 512:(c + 1) * 512]
                    sp.dma_start(ring[:, s, :].rearrange("p (k n) -> p k n", n=512),
                                 src.rearrange("(k p) n -> p k n", p=P)).then_inc(landed[s], 16)

            for l in range(L):
                for n, u in enumerate(UNITS):
                    if n >= RING:
                        wait_mixing(l, UNITS[n - RING])
                    elif l > 0:
                        wait_pair(l - 1, NP - 1, n + 16)
                    src = unit_source(l, u)
                    k, width = src.shape[1], src.shape[2]
                    sp.dma_start(ring[:, n % RING, 0:k * width].rearrange("p (k n) -> p k n", n=width) if width != 416
                                 else ring[:, n % RING, :].rearrange("p (k n) -> p k n", n=512)[:, :, 0:416],
                                 src).then_inc(landed[n % RING], 16)
                load_pair(l, 0, True)
                with sp.Fori(1, NP) as pr:
                    load_pair(l, pr, False)
            x_final(sp, L - 1)
            sp.dma_start(outs[0][0], x[:, 0, :]).then_inc(out_done, 16)
            sp.dma_start(outs[1][0].rearrange("(t p) d -> p t d", p=P), x[:, 1:3, :]).then_inc(out_done, 16)
            sp.wait_ge(out_done, 32)
            sp.wait_ge(cache_out, 64 * L)

        @block.gpsimd
        def _(pool):
            step = steps(pool, pool_step)
            step(nc.gpsimd.memset(mhalf[:, :], -0.5))
            nc.gpsimd.memset(kTp[:, :, :], 0.0).then_inc(pads_zero, 1)
            nc.gpsimd.memset(xcur[:, :, :, :], 0.0).then_inc(pads_zero, 1)
            events = [0]

            def power(c0, n):
                events[0] += 1
                pool.wait_ge(var_ready, events[0])
                nc.gpsimd.tensor_tensor(rstd[:, c0:c0 + n], var[:, c0:c0 + n], mhalf[:, 0:n], ALU.pow)\
                    .then_inc(rstd_ready, 1)

            for l in range(L):
                if l == 0:
                    pool.wait_ge(pads_zero, 1)
                else:
                    x_final(pool, l - 1)
                loads = [
                    (rows[:, :], a["rows"][l].partition_broadcast(P)),
                    (poolw, a["pool_w"][l].rearrange("g c d -> c g d")),
                    (inv.rearrange("p g t -> p (g t)"), a["counts"][0].partition_broadcast(P)),
                    (wrout[:, :, :], a["w_router"][l].rearrange("(k p) e -> p k e", p=P)),
                    (kTp[0:SD, 0, TOK:512], a["ctx_kT"][l, 0:SD, :]),
                    (kTp[SD:P, 1, TOK:512], a["ctx_kT"][l, SD:P, :]),
                    (vtok[:, 3, :], a["ctx_v"][l]),
                    (ckvT[:, :, TOK:512], a["ctx_ckvT"][l].rearrange("(k p) t -> p k t", p=P)),
                    (kr[:, 3, :], a["ctx_kr"][l]),
                ]
                assert len(loads) == 9
                for dst, src in loads:
                    pool.dma_start(dst, src).then_inc(layer_in, 16)
                for lo, hi in ((0, 8), (136, 152), (408, 416)):
                    step(nc.gpsimd.memset(upad[:, :, lo:hi], 0.0))
                power(0, 3)
                for t in range(T):
                    power(3 + 8 * t, 8)
                for t in range(T):
                    power(27 + 4 * t, 4)
                pool.wait_ge(layer_in, 16 * 9 * (l + 1))
                for g in range(4):
                    wait_read(pool, l, ("u", g))
                    src, w = upad[:, g, :], 1
                    for k in range(g + 1):
                        dst = win[:, k % 2, :]
                        back, ahead = (1, 0) if k == 0 else (w // 2, w // 2)
                        m = 2 ** g - 2 ** k
                        lo, hi = 8 - m, 408 + m
                        step(nc.gpsimd.tensor_tensor(dst[:, lo:hi], src[:, lo - back:hi - back],
                                                     src[:, lo + ahead:hi + ahead], ALU.add))
                        src, w = dst, 2 * w
                    for p0, t0, n in PSEG:
                        step(nc.gpsimd.tensor_tensor(yaT[:, g, t0:t0 + n], src[:, p0:p0 + n], inv[:, g, t0:t0 + n], ALU.mult))
                    for p0, t0, n in PSEG:
                        nc.gpsimd.tensor_tensor(yaT[:, g, t0:t0 + n], yaT[:, g, t0:t0 + n], upad[:, g, p0:p0 + n],
                                                ALU.subtract).then_inc(pool_ready, 1)
                    pool.wait_ge(pool_ready, 8 * l + 2 * g + 2)
                for t in range(T):
                    power(39 + 8 * t, 8)
                for t in range(4):
                    power(63 + 8 * t, 8)
                wait_full(pool, l, ("o", 7))
                pool.dma_start(gb, a["b_mod"][l, 2 * D:3 * D].partition_broadcast(P)).then_inc(gate_row_in, 16)
                pool.dma_start(gb2, a["b_mod"][l, 5 * D:6 * D].partition_broadcast(P)).then_inc(gate_row_in, 16)
                power(95, 3)
                wait_read(pool, l, ("selt", NP - 2))
                wait_read(pool, l, ("selt", NP - 1))
                wait_read(pool, l, ("gather", KB - 1, 0))
                wait_read(pool, l, ("gather", KB - 1, 1))
                with pool.Fori(0, NP) as pr:
                    b = BANK_U[1]
                    pool.wait_ge(bank_full[b], l * BANKS[b] + MIXED[b] + pr)
                    for e in range(2):
                        nc.gpsimd.tensor_copy(xcur[:, e, :, 0:USED],
                                              xg[:, :, bass.ds(2 * pr + e, 1), :].rearrange("p k q s -> p k (q s)"))\
                            .then_inc(xcur_ready, 1)
                    for b in (BANK_T, BANK_Y):
                        pool.wait_ge(bank_full[b], l * BANKS[b] + MIXED[b] + pr * PAIR[b])
                    nc.gpsimd.tensor_copy(selcur, selT[:, bass.ds(pr, 1), :].rearrange("p q t -> p (q t)"))\
                        .then_inc(selcur_ready, 1)

        @block.scalar
        def _(act):
            step = steps(act, act_step)
            F = nc.scalar.activation
            act.wait_ge(const_in, 48)
            F(cs[:, :, :], cond, ACT.Tanh, scale=0.5).then_inc(cond_tanh, 1)
            sq = [0]

            def square(src, c0, n, more):
                b = sq[0] % 2
                if sq[0] >= 2:
                    act.wait_ge(sq_used, sq[0] - 1)
                dst = sqb[:, b, c0:c0 + n]
                if len(src.shape) == 3:
                    dst = dst.rearrange("p (h d) -> p h d", d=src.shape[2])
                ins = F(dst, src, ACT.Square)
                if more:
                    step(ins)
                else:
                    ins.then_inc(sq_ready, 1)
                    sq[0] += 1

            def x_stats(l, c0):
                for t in range(T):
                    if xs[0]:
                        act.wait_ge(xss_ready, xs[0])
                    F(junk, x[:, t, :], ACT.Square, accum_out=ss[:, c0 + t:c0 + t + 1]).then_inc(xss_ready, 1)
                    xs[0] += 1
            xs = [0]

            def mod_row(l, i):
                ps = wait_full(act, l, ("mod", i))
                read(l, ("mod", i), F(modrow[:, i % 2, :], ps[:, :], ACT.Copy))

            def h_evac(l, name, kb):
                ps = wait_full(act, l, (name, kb))
                step(F(hT[:, kb, 0:P], ps[:, 0:P], ACT.Identity, scale=amp[:, kb, 0:1], bias=shift[:, kb, 0:1]))
                read(l, (name, kb), F(hT[:, kb, P:TOK], ps[:, P:TOK], ACT.Identity, scale=amp[:, kb, 1:2],
                                      bias=shift[:, kb, 1:2]))

            def exps(l, i):
                s = i % 2
                scale = SD ** -0.5 if i < SH else MQ ** -0.5
                act.wait_ge(negm_ready, 16 * l + i + 1)
                sa, _ = turn(l, ("sa", i))
                sbk, _ = turn(l, ("sb", i))
                step(F(prob[:, s, 0:P], bank[sa][:, 0:P], ACT.Exp, bias=negm[:, s, 0:1], scale=scale,
                       accum_out=rsum[:, s, 0:1]))
                read(l, ("sa", i), F(prob[:, s, P:512], bank[sa][:, P:512], ACT.Exp, bias=negm[:, s, 1:2], scale=scale,
                                     accum_out=rsum[:, s, 1:2]))
                if i < SH:
                    F(esink[:, s, :], negm[:, s, :], ACT.Exp, bias=rows[:, ROW_SINK + i:ROW_SINK + i + 1])\
                        .then_inc(sink_ready, 1)
                read(l, ("sb", i), F(prob[:, s, 512:896], bank[sbk][:, 0:TOK], ACT.Exp, bias=negm[:, s, 2:3],
                                     scale=scale, accum_out=rsum[:, s, 2:3]))

            def gate_tanh(l, b, j):
                ps = wait_full(act, l, ("gate", b, j))
                if 8 * b + j >= 2:
                    act.wait_ge(merged_ready, 24 * l + 8 * b + j - 1)
                read(l, ("gate", b, j), F(tanh_g[:, j % 2, :], ps[:, 0:TOK], ACT.Tanh, scale=0.5))

            for l in range(L):
                if l == 0:
                    act.wait_ge(x_in, 32)
                else:
                    x_final(act, l - 1)
                x_stats(l, 0)
                for i in range(4):
                    mod_row(l, i)
                act.wait_ge(cols_ready, 2 * l + 1)
                for kb in range(1, KB, 2):
                    h_evac(l, "h1", kb)
                for t in range(T):
                    square(wait_full(act, l, ("seg", 0, t))[:, :], 0, 512, False)
                for t in range(T):
                    ps = wait_full(act, l, ("seg", 1, t))
                    square(ps[:, 0:P], 0, P, False)
                    step(F(vtok[:, t, :], ps[:, P:2 * P], ACT.Copy))
                    F(qctok[:, t, 0:256], ps[:, 256:512], ACT.Copy).then_inc(cseg_read, 1)
                act.wait_ge(layer_in, 16 * 9 * (l + 1))
                for t in range(T):
                    ps = wait_full(act, l, ("seg", 2, t))
                    step(F(qctok[:, t, 256:QR], ps[:, 0:P], ACT.Copy))
                    c0 = 27 + 4 * t
                    act.wait_ge(cseg_read, 3 * l + t + 1)
                    step(F(yaT[:, 0, 0:QR], qctok[:, t, :], ACT.Square, accum_out=ss[:, c0 + 2:c0 + 3]))
                    step(F(yaT[:, 1, 0:KVR], ps[:, P:QR], ACT.Square, accum_out=ss[:, c0 + 3:c0 + 4]))
                    step(F(kr[:, t, :], ps[:, QR:QR + ROPE], ACT.Copy))
                    F(yaT[:, 2, 32 * t:32 * t + ROPE], kr[:, t, :], ACT.Square, accum_out=sskr[:, t:t + 1])\
                        .then_inc(dseg_read, 1)
                F(yaT[:, 3, 0:ROPE], kr[:, 3, :], ACT.Square, accum_out=sskr[:, 3:4]).then_inc(dseg_read, 1)
                for g in range(4):
                    ps = wait_full(act, l, ("u", g))
                    step(F(upad[:, g, 8:8 + P], ps[:, 0:P], ACT.Copy))
                    read(l, ("u", g), F(upad[:, g, 152:408], ps[:, P:TOK], ACT.Copy))
                for dst, src, s in ((outs[2][0, l], ktok[:, 0, :], ktok_ready), (outs[3][0, l], vtok[:, 0, :], None),
                                    (outs[4][0, l], ckvtok[:, 0, :], ckvtok_ready), (outs[5][0, l], kr[:, 0, :], None)):
                    if s is not None:
                        act.wait_ge(s, 3 * l + 1)
                    act.dma_start(dst, src).then_inc(cache_out, 16)
                for t in range(T):
                    ps = wait_full(act, l, ("tq", t))
                    read(l, ("tq", t), F(qT[:, :, t * P:(t + 1) * P], ps[:, :].rearrange("p (b t) -> p b t", t=P), ACT.Copy))
                for t in range(T):
                    ps = wait_full(act, l, ("tkc", t))
                    if l == 0 and t == 0:
                        act.wait_ge(pads_zero, 1)
                    step(F(kTp[0:SD, 0, t * P:(t + 1) * P], ps[0:SD, 0:P], ACT.Copy))
                    step(F(kTp[SD:P, 1, t * P:(t + 1) * P], ps[SD:P, 0:P], ACT.Copy))
                    read(l, ("tkc", t), F(qcT[:, :, t * P:(t + 1) * P], ps[:, P:512].rearrange("p (b t) -> p b t", t=P),
                                          ACT.Copy))
                ps = wait_full(act, l, ("tkv", 0))
                for t in range(2):
                    ins = F(ckvT[:, :, t * P:(t + 1) * P],
                            ps[:, t * 256:(t + 1) * 256].rearrange("p (b t) -> p b t", t=P), ACT.Copy)
                    if t == 0:
                        step(ins)
                    else:
                        read(l, ("tkv", 0), ins)
                ps = wait_full(act, l, ("tkv", 1))
                read(l, ("tkv", 1), F(ckvT[:, :, 2 * P:TOK], ps[:, 0:256].rearrange("p (b t) -> p b t", t=P), ACT.Copy))
                for t in range(T):
                    for h in range(2):
                        ps = wait_full(act, l, ("wq", h, t))
                        square(ps[:, 0:QR], h * QR, QR, h == 0)
                for g in range(4):
                    ps = wait_full(act, l, ("pool", g))
                    read(l, ("pool", g), F(yaT[:, g, :], ps[:, 0:TOK], ACT.Copy, scale=cols[:, l, COL_PS + g:COL_PS + g + 1]))
                act.wait_ge(cache_out, 64 * (l + 1))
                for t in range(4):
                    for h in range(2):
                        ps = wait_full(act, l, ("wkv", t, h))
                        square(ps[:, :].rearrange("p (h c) -> p h c", c=P)[:, :, 0:NOPE], h * 256, 256, h == 0)
                        F(vm[:, t, 4 * h:4 * h + 4, :], ps[:, :].rearrange("p (h c) -> p h c", c=P)[:, :, NOPE:P],
                          ACT.Copy).then_inc(v_read, 1)
                    if t < 3:
                        for h in range(2):
                            ps = wait_full(act, l, ("tqm", t, h))
                            read(l, ("tqm", t, h), F(qmT[0:MQ, 4 * h:4 * h + 4, t * P:(t + 1) * P],
                                                     ps[0:MQ, :].rearrange("p (h t) -> p h t", t=P), ACT.Copy))
                for t in range(4):
                    for h in range(2):
                        ps = wait_full(act, l, ("tkm", t, h))
                        read(l, ("tkm", t, h), F(kmT[0:MQ, 4 * h:4 * h + 4, t * P:(t + 1) * P],
                                                 ps[0:MQ, :].rearrange("p (h t) -> p h t", t=P), ACT.Copy))
                exps(l, 0)
                for i in range(SH + MH):
                    if i < 15:
                        exps(l, i + 1)
                    gate_tanh(l, i // 8, i % 8)
                    ps = wait_full(act, l, ("x", i))
                    read(l, ("x", i), F(probT[:, i % 2, 0:4, :], ps[:, :].rearrange("p (b t) -> p b t", t=P), ACT.Copy))
                    if i % 2:
                        ps = wait_full(act, l, ("o", i // 2))
                        y = ybT if i < 8 else yaT
                        j = (i // 2) % 4
                        read(l, ("o", i // 2), F(y[:, j, :], ps[:, 0:TOK], ACT.Copy))
                for i in (4, 5):
                    mod_row(l, i)
                for j in range(KB):
                    gate_tanh(l, 2, j)
                for t in range(T):
                    act.wait_ge(x_mixed, 3 * l + t + 1)
                    act.wait_ge(xss_ready, xs[0])
                    F(junk, x[:, t, :], ACT.Square, accum_out=ss[:, 95 + t:96 + t]).then_inc(xss_ready, 1)
                    xs[0] += 1
                for i in range(6, 12):
                    mod_row(l, i)
                act.wait_ge(cols_ready, 2 * l + 2)
                for kb in range(1, KB, 2):
                    h_evac(l, "h2", kb)
                act.wait_ge(exp_in_ready, l + 1)
                F(aff, logit, ACT.Exp).then_inc(exp_ready, 1)
                for kb in range(KB):
                    ps = wait_full(act, l, ("gather", kb, 1))
                    v = ps[:, 0:8 * USED].rearrange("p (e s) -> p e s", s=USED)
                    step(F(xg[:, kb, 8:16, 0:CP], v[:, :, 0:CP], ACT.Identity, scale=amp[:, kb, 0:1], bias=shift[:, kb, 0:1]))
                    read(l, ("gather", kb, 1), F(xg[:, kb, 8:16, CP:USED], v[:, :, CP:USED], ACT.Identity,
                                                 scale=amp[:, kb, 1:2], bias=shift[:, kb, 1:2]))
                for pr in range(1, NP, 2):
                    ps = wait_full(act, l, ("selt", pr))
                    read(l, ("selt", pr), F(selT[:, pr, :], ps[:, 0:TOK], ACT.Copy))
                with act.Fori(0, NP) as pr:
                    for h in range(2):
                        b = BANK_G[h]
                        act.wait_ge(bank_full[b], l * BANKS[b] + MIXED[b] + pr + 1)
                        F(th[h], bank[b][:, :], ACT.Tanh, scale=0.5).then_inc(th_ready, 1)
                    for h in range(2):
                        n = l * BANKS[BANK_T] + MIXED[BANK_T] + pr * 5 + h
                        act.wait_ge(bank_full[BANK_T], n + 1)
                        F(hidT[:, 4 * h:4 * h + 4, :], bank[BANK_T][:, :].rearrange("p (b t) -> p b t", t=P), ACT.Copy)\
                            .then_inc(bank_read[BANK_T], 1)

        @block.vector
        def _(dve):
            V = nc.vector
            step = steps(dve, dve_step)
            ev = [0]
            sq = [0]

            def variance(c0, n, width, last=True):
                ins = V.tensor_scalar(var[:, c0:c0 + n], ss[:, c0:c0 + n], 1.0 / width, EPS, ALU.mult, ALU.add)
                if last:
                    ins.then_inc(var_ready, 1)
                else:
                    step(ins)

            def wait_rstd():
                ev[0] += 1
                dve.wait_ge(rstd_ready, ev[0])

            def reduce_squares(h, d, c0):
                dve.wait_ge(sq_ready, sq[0] + 1)
                V.reduce_sum(ss[:, c0:c0 + h], sqb[:, sq[0] % 2, 0:h * d].rearrange("p (h d) -> p h d", d=d), axis=AX)\
                    .then_inc(sq_used, 1)
                sq[0] += 1
                dve.wait_ge(sq_used, sq[0])

            def rotate(v, heads, width, table, last):
                q = width // 4
                n = heads * width
                ra = ropea[:, 0:n].rearrange("p (h d) -> p h d", d=width)
                rb = ropeb[:, 0:n].rearrange("p (h d) -> p h d", d=width)
                cos = table[:, 0, :].unsqueeze(1).to_broadcast([P, heads, width])
                step(V.tensor_tensor(ra, v, cos, ALU.mult))
                sin = table[:, 1, :].rearrange("p (x y f) -> p x y f", y=2, f=q)
                for half in range(2):
                    v5 = v.rearrange("p h (x y f) -> p h x y f", y=2, f=q)[:, :, :, 1 - half, :]
                    o5 = rb.rearrange("p h (x y f) -> p h x y f", y=2, f=q)[:, :, :, half, :]
                    s5 = sin[:, :, half, :].unsqueeze(1).to_broadcast([P, heads, 2, q])
                    step(V.tensor_tensor(o5, v5, s5, ALU.mult))
                last(V.tensor_tensor(v, ra, rb, ALU.add))

            def heads_norm(v, src, r0, heads, width):
                step(V.tensor_tensor(v, src, rstd[:, r0:r0 + heads].unsqueeze(2).to_broadcast([P, heads, width]), ALU.mult))

            def normalise(l, c0):
                for t in range(T):
                    V.tensor_scalar(xn[:, t, :], x[:, t, :], rstd[:, c0 + t:c0 + t + 1], None, ALU.mult)\
                        .then_inc(xn_ready, 1)

            def mod_cols(l, k):
                ps = wait_full(dve, l, ("modcol", k))
                v = ps[:, 0:32].rearrange("p (b s) -> p b s", s=2)
                b0, g0 = COL_B + 24 * k, (COL_N1, COL_N2)[k]

                def col(c):
                    return cols[:, l, c:c + KB].unsqueeze(2).to_broadcast([P, KB, 2])
                step(V.tensor_tensor(shift[:, :, :], v[:, 0:KB, :], col(b0), ALU.add))
                b, n = turn(l, ("modcol", k))
                V.tensor_tensor(amp[:, :, :], v[:, KB:2 * KB, :], col(b0 + KB), ALU.add).then_inc(bank_read[b], 1)
                dve.wait_ge(bank_read[b], n + 1)
                step(V.tensor_scalar(amp[:, :, :], amp[:, :, :], 1.0, None, ALU.add))
                V.tensor_tensor(amp[:, :, :], amp[:, :, :], col(g0), ALU.mult).then_inc(cols_ready, 1)
                dve.wait_ge(cols_ready, 2 * l + k + 1)

            def h_evac(l, name, kb):
                ps = wait_full(dve, l, (name, kb))
                step(V.tensor_scalar(hT[:, kb, 0:P], ps[:, 0:P], amp[:, kb, 0:1], shift[:, kb, 0:1], ALU.mult, ALU.add))
                read(l, (name, kb), V.tensor_scalar(hT[:, kb, P:TOK], ps[:, P:TOK], amp[:, kb, 1:2], shift[:, kb, 1:2],
                                                    ALU.mult, ALU.add))

            def merge(l, b, j):
                ps = wait_full(dve, l, ("br", b, j))
                wait_read(dve, l, ("gate", b, j))
                dst = merged[:, j, :] if b == 0 else gated
                V.scalar_tensor_tensor(dst, tanh_g[:, j % 2, :], 1.0, ps[:, 0:TOK], ALU.add, ALU.mult)\
                    .then_inc(bank_read[turn(l, ("br", b, j))[0]], 1)
                wait_read(dve, l, ("br", b, j))
                if b:
                    V.tensor_tensor(merged[:, j, :], merged[:, j, :], gated, ALU.add).then_inc(merged_ready, 1)
                else:
                    dve.sem_inc(merged_ready, 1)
                dve.wait_ge(merged_ready, 24 * l + 8 * b + j + 1)

            def maxima(l, i):
                s = i % 2
                sa, sbk = wait_full(dve, l, ("sa", i)), wait_full(dve, l, ("sb", i))
                if i < SH:
                    step(V.tensor_tensor(sa[:, 256:TOK], sa[:, 256:TOK], band[:, 0, :], ALU.add))
                    step(V.tensor_tensor(sbk[:, 0:P], sbk[:, 0:P], band[:, 1, :], ALU.add))
                step(V.reduce_max(mx[:, s, 0:1], sa[:, 0:P], axis=AX))
                step(V.reduce_max(mx[:, s, 1:2], sa[:, P:512], axis=AX))
                step(V.reduce_max(mx[:, s, 2:3], sbk[:, 0:TOK], axis=AX))
                if i < SH:
                    ins = V.tensor_scalar(negm[:, s, :], mx[:, s, :], -SD ** -0.5, negsink[:, i:i + 1], ALU.mult, ALU.min)
                else:
                    ins = V.tensor_scalar(negm[:, s, :], mx[:, s, :], -MQ ** -0.5, None, ALU.mult)
                ins.then_inc(negm_ready, 1)

            def divide(l, i):
                s = i % 2
                wait_read(dve, l, ("sb", i))
                den = rsum[:, s, :]
                if i < SH:
                    dve.wait_ge(sink_ready, SH * l + i + 1)
                    step(V.tensor_tensor(esink[:, s, :], esink[:, s, :], rsum[:, s, :], ALU.add))
                    den = esink[:, s, :]
                step(V.reciprocal(rinv[:, s, :], den))
                for n, (lo, hi) in enumerate(((0, P), (P, 512), (512, 896))):
                    V.tensor_scalar(prob[:, s, lo:hi], prob[:, s, lo:hi], rinv[:, s, n:n + 1], None, ALU.mult)\
                        .then_inc(prob_ready, 1)

            dve.wait_ge(cond_tanh, 1)
            step(V.scalar_tensor_tensor(cs[:, :, :], cs[:, :, :], 1.0, cond, ALU.add, ALU.mult))
            V.tensor_scalar(cs[:, :, :], cs[:, :, :], 0.5, None, ALU.mult).then_inc(cond_ready, 1)

            for l in range(L):
                dve.wait_ge(xss_ready, 6 * l + 3)
                variance(0, 3, D)
                wait_rstd()
                normalise(l, 0)
                mod_cols(l, 0)
                for kb in range(0, KB, 2):
                    h_evac(l, "h1", kb)
                dve.wait_ge(layer_in, 16 * 9 * (l + 1))
                step(V.tensor_scalar(negsink[:, :], rows[:, ROW_SINK:NROW], -1.0, None, ALU.mult))

                def row(c, heads, width):
                    return rows[:, c:c + width].unsqueeze(1).to_broadcast([P, heads, width])
                for t in range(T):
                    reduce_squares(SH, SD, 3 + 8 * t)
                    variance(3 + 8 * t, 8, SD)
                for t in range(T):
                    wait_rstd()
                    q = qtok[:, t, :].rearrange("p (h d) -> p h d", d=SD)
                    b, n = turn(l, ("seg", 0, t))
                    V.tensor_tensor(qtok[:, t, :].rearrange("p (b j d) -> p j b d", j=2, d=SD),
                                    bank[b][:, :].rearrange("p (j b d) -> p j b d", j=2, d=SD),
                                    rstd[:, 3 + 8 * t:11 + 8 * t].rearrange("p (j b) -> p j b", j=2).unsqueeze(3)
                                    .to_broadcast([P, 2, 4, SD]), ALU.mult)\
                        .then_inc(bank_read[b], 1)
                    dve.wait_ge(bank_read[b], n + 1)
                    ins = V.tensor_tensor(q, q, row(ROW_QG, SH, SD), ALU.mult)
                    if t == 0:
                        ins.then_inc(qtok_ready, 1)
                    else:
                        step(ins)
                        rotate(q, SH, SD, ropes[:, t - 1, :, :], lambda i: i.then_inc(qtok_ready, 1))
                for t in range(T):
                    c0 = 27 + 4 * t
                    reduce_squares(2, SD, c0)
                    dve.wait_ge(dseg_read, 4 * l + t + 1)
                    variance(c0, 2, SD, False)
                    variance(c0 + 2, 1, QR, False)
                    variance(c0 + 3, 1, KVR)
                for t in range(T):
                    c0 = 27 + 4 * t
                    wait_rstd()
                    k = ktok[:, t, :].rearrange("p (h d) -> p h d", d=SD)
                    b, n = turn(l, ("seg", 1, t))
                    dve.wait_ge(cseg_read, 3 * l + t + 1)
                    V.tensor_tensor(k, bank[b][:, 0:P].rearrange("p (h d) -> p h d", d=SD),
                                    rstd[:, c0:c0 + 2].unsqueeze(2).to_broadcast([P, 2, SD]), ALU.mult)\
                        .then_inc(bank_read[b], 1)
                    dve.wait_ge(bank_read[b], n + 1)
                    ins = V.tensor_tensor(k, k, row(ROW_KG, 2, SD), ALU.mult)
                    if t == 0:
                        ins.then_inc(ktok_ready, 1)
                    else:
                        step(ins)
                        rotate(k, 2, SD, ropes[:, t - 1, :, :], lambda i: i.then_inc(ktok_ready, 1))
                    V.scalar_tensor_tensor(qctok[:, t, :], qctok[:, t, :], rstd[:, c0 + 2:c0 + 3],
                                           rows[:, ROW_QCG:ROW_QCG + QR], ALU.mult, ALU.mult).then_inc(qctok_ready, 1)
                    b, n = turn(l, ("seg", 2, t))
                    V.scalar_tensor_tensor(ckvtok[:, t, :], bank[b][:, P:QR], rstd[:, c0 + 3:c0 + 4],
                                           rows[:, ROW_KVG:ROW_KVG + KVR], ALU.mult, ALU.mult).then_inc(ckvtok_ready, 1)
                    dve.wait_ge(ckvtok_ready, 3 * l + t + 1)
                    dve.sem_inc(bank_read[b], 1)
                dve.wait_ge(dseg_read, 4 * l + 4)
                step(V.tensor_tensor(krg[:, :, :], kr[:, :, :], row(ROW_MKG + NOPE, 4, ROPE), ALU.mult))
                for t in (1, 2):
                    rotate(krg[:, t:t + 1, :], 1, ROPE, ropem[:, t - 1, :, :], step)
                for t in range(T):
                    c0 = 39 + 8 * t
                    reduce_squares(MH, MQ, c0)
                    variance(c0, 8, MQ)
                    wait_rstd()
                    if t == 2:
                        wait_full(dve, l, ("tqm", 0, 1))
                    v = tok[:, t % 2, :].rearrange("p (h d) -> p h d", d=MQ)
                    for h in range(2):
                        b, n = turn(l, ("wq", h, t))
                        V.tensor_tensor(v[:, 4 * h:4 * h + 4, :], bank[b][:, 0:QR].rearrange("p (h d) -> p h d", d=MQ),
                                        rstd[:, c0 + 4 * h:c0 + 4 * h + 4].unsqueeze(2).to_broadcast([P, 4, MQ]),
                                        ALU.mult).then_inc(bank_read[b], 1)
                        dve.wait_ge(bank_read[b], n + 1)
                    ins = V.tensor_tensor(v, v, row(ROW_MQG, MH, MQ), ALU.mult)
                    if t == 0:
                        ins.then_inc(tok_ready, 1)
                    else:
                        step(ins)
                        rotate(v[:, :, NOPE:MQ], MH, ROPE, ropem[:, t - 1, :, :], lambda i: i.then_inc(tok_ready, 1))
                for t in range(4):
                    c0 = 63 + 8 * t
                    reduce_squares(MH, NOPE, c0)
                    step(V.tensor_scalar(ss[:, c0:c0 + 8], ss[:, c0:c0 + 8], sskr[:, t:t + 1], None, ALU.add))
                    variance(c0, 8, MQ)
                    wait_rstd()
                    wait_full(dve, l, [("tqm", 1, 1), ("tqm", 2, 1), ("tkm", 0, 1), ("tkm", 1, 1)][t])
                    v = tok[:, (3 + t) % 2, :].rearrange("p (h d) -> p h d", d=MQ)
                    for h in range(2):
                        b, n = turn(l, ("wkv", t, h))
                        dve.wait_ge(v_read, 8 * l + 2 * t + h + 1)
                        V.tensor_tensor(v[:, 4 * h:4 * h + 4, 0:NOPE],
                                        bank[b][:, :].rearrange("p (h c) -> p h c", c=P)[:, :, 0:NOPE],
                                        rstd[:, c0 + 4 * h:c0 + 4 * h + 4].unsqueeze(2).to_broadcast([P, 4, NOPE]),
                                        ALU.mult).then_inc(bank_read[b], 1)
                        dve.wait_ge(bank_read[b], n + 1)
                    step(V.tensor_tensor(v[:, :, 0:NOPE], v[:, :, 0:NOPE], row(ROW_MKG, MH, NOPE), ALU.mult))
                    V.tensor_tensor(v[:, :, NOPE:MQ], krg[:, t, :].unsqueeze(1).to_broadcast([P, MH, ROPE]),
                                    rstd[:, c0:c0 + 8].unsqueeze(2).to_broadcast([P, MH, ROPE]), ALU.mult)\
                        .then_inc(tok_ready, 1)
                maxima(l, 0)
                for i in range(SH + MH):
                    divide(l, i)
                    if i < 15:
                        maxima(l, i + 1)
                    ps = wait_full(dve, l, ("y", i))
                    read(l, ("y", i), V.tensor_copy(probT[:, i % 2, 4:7, :], ps[:, 0:TOK].rearrange("p (b t) -> p b t", t=P)))
                    merge(l, i // 8, i % 8)
                dve.wait_ge(gate_row_in, 32 * (l + 1))
                for i in (4, 5):
                    for v in range(2):
                        ps = wait_full(dve, l, ("modb", i, v))
                        c = (i - 4) * 512
                        V.tensor_tensor(g1b[:, v, c:c + 512], ps[:, :], gb[:, c:c + 512], ALU.add)\
                            .then_inc(bank_read[turn(l, ("modb", i, v))[0]], 1)
                        wait_read(dve, l, ("modb", i, v))
                step(V.tensor_scalar(g1b, g1b, 0.5, None, ALU.mult))
                for j in range(KB):
                    merge(l, 2, j)
                for n in range(2):
                    for t in range(T):
                        ps = wait_full(dve, l, ("wo", n, t))
                        V.tensor_tensor(wtmp[:, t % 2, :], ps[:, :], g1b[:, min(t, 1), n * 512:(n + 1) * 512], ALU.mult)\
                            .then_inc(bank_read[turn(l, ("wo", n, t))[0]], 1)
                        wait_read(dve, l, ("wo", n, t))
                        xs = x[:, t, n * 512:(n + 1) * 512]
                        ins = V.tensor_tensor(xs, xs, wtmp[:, t % 2, :], ALU.add)
                        if n:
                            ins.then_inc(x_mixed, 1)
                        else:
                            step(ins)
                dve.wait_ge(xss_ready, 6 * l + 6)
                variance(95, 3, D)
                wait_rstd()
                normalise(l, 95)
                mod_cols(l, 1)
                for i in (10, 11):
                    ps = wait_full(dve, l, ("modb", i, 0))
                    c = (i - 10) * 512
                    V.tensor_tensor(g2slot[:, c:c + 512], ps[:, :], gb2[:, c:c + 512], ALU.add)\
                        .then_inc(bank_read[turn(l, ("modb", i, 0))[0]], 1)
                for kb in range(0, KB, 2):
                    h_evac(l, "h2", kb)
                ps = wait_full(dve, l, ("route", 0))
                lg = ps[:, 0:T * NE].rearrange("p (t e) -> p t e", e=NE)
                step(V.reduce_max(small[:, 0:3], lg, axis=AX))
                b, n = turn(l, ("route", 0))
                V.tensor_tensor(logit, lg, small[:, 0:3].unsqueeze(2).to_broadcast([P, T, NE]), ALU.subtract)\
                    .then_inc(bank_read[b], 1)
                dve.wait_ge(bank_read[b], n + 1)
                dve.sem_inc(exp_in_ready, 1)
                dve.wait_ge(exp_ready, l + 1)
                step(V.reduce_sum(small[:, 3:6], aff, axis=AX))
                step(V.reciprocal(small[:, 6:9], small[:, 3:6]))
                V.tensor_tensor(aff, aff, small[:, 6:9].unsqueeze(2).to_broadcast([P, T, NE]), ALU.mult)\
                    .then_inc(aff_ready, 1)
                ps = wait_full(dve, l, ("afft", 0))
                b, n = turn(l, ("afft", 0))
                step(V.tensor_copy(affT[0:NE, :], ps[0:NE, 0:TOK]))
                V.tensor_copy(work[0:NE, :], ps[0:NE, 0:TOK]).then_inc(bank_read[b], 1)
                dve.wait_ge(bank_read[b], n + 1)
                for lo, hi, cap in ((0, P, CP), (P, TOK, CS)):
                    for r in range(cap // 8):
                        if r:
                            step(V.match_replace(work[0:NE, lo:hi], top8[0:NE, :], work[0:NE, lo:hi], -1.0))
                        step(V.max(top8[0:NE, :], work[0:NE, lo:hi]))
                    for k, op in enumerate((ALU.is_gt, ALU.is_equal)):
                        ins = V.tensor_scalar(ge[0:NE, k * TOK + lo:k * TOK + hi], affT[0:NE, lo:hi], top8[0:NE, 7:8], None, op)
                        if lo and k:
                            ins.then_inc(ge_ready, 1)
                        else:
                            step(ins)
                ps = wait_full(dve, l, ("get", 0))
                b, n = turn(l, ("get", 0))
                V.tensor_copy(get, ps[:, 0:T * 2 * NE].rearrange("p (t k) -> p t k", k=2 * NE)).then_inc(bank_read[b], 1)
                dve.wait_ge(bank_read[b], n + 1)
                ps = wait_full(dve, l, ("cum", 0))
                cum = ps[:, 0:T * 2 * NE].rearrange("p (t k) -> p t k", k=2 * NE)
                step(V.tensor_tensor(sl1, get[:, :, 0:NE], cum[:, :, 0:NE], ALU.mult))
                b, n = turn(l, ("cum", 0))
                V.tensor_tensor(sl2, get[:, :, NE:2 * NE], cum[:, :, NE:2 * NE], ALU.mult).then_inc(bank_read[b], 1)
                dve.wait_ge(bank_read[b], n + 1)
                step(V.tensor_tensor(sl1, sl1, sl2, ALU.add))
                step(V.tensor_tensor(sl2, get[:, :, 0:NE], get[:, :, NE:2 * NE], ALU.add))
                step(V.scalar_tensor_tensor(sl1, sl2, -BIG, sl1, ALU.mult, ALU.add))
                step(V.tensor_scalar(sl1, sl1, BIG, None, ALU.add))
                for t in range(T):
                    V.tensor_tensor(sel[:, t, :].rearrange("p (e s) -> p e s", s=SLOTS),
                                    sl1[:, t, :].unsqueeze(2).to_broadcast([P, NE, SLOTS]),
                                    slotno[:, min(t, 1), :].unsqueeze(1).to_broadcast([P, NE, SLOTS]), ALU.is_equal)\
                        .then_inc(sel_ready, 1)
                for kb in range(KB):
                    ps = wait_full(dve, l, ("gather", kb, 0))
                    v = ps[:, 0:8 * USED].rearrange("p (e s) -> p e s", s=USED)
                    step(V.tensor_scalar(xg[:, kb, 0:8, 0:CP], v[:, :, 0:CP], amp[:, kb, 0:1], shift[:, kb, 0:1],
                                         ALU.mult, ALU.add))
                    read(l, ("gather", kb, 0), V.tensor_scalar(xg[:, kb, 0:8, CP:USED], v[:, :, CP:USED], amp[:, kb, 1:2],
                                                               shift[:, kb, 1:2], ALU.mult, ALU.add))
                wait_full(dve, l, ("gather", KB - 1, 1))
                for t in range(T):
                    v = sel[:, t, :].rearrange("p (e s) -> p e s", s=SLOTS)
                    V.tensor_tensor(v, v, aff[:, t, :].unsqueeze(2).to_broadcast([P, NE, SLOTS]), ALU.mult)\
                        .then_inc(selv_ready, 1)
                for pr in range(0, NP, 2):
                    ps = wait_full(dve, l, ("selt", pr))
                    read(l, ("selt", pr), V.tensor_copy(selT[:, pr, :], ps[:, 0:TOK]))
                with dve.Fori(0, NP) as pr:
                    for h in range(2):
                        k = l * 2 * NP + pr * 2 + h
                        dve.wait_ge(th_ready, k + 1)
                        V.scalar_tensor_tensor(s1, th[h], 1.0, bank[BANK_G[h]][:, :], ALU.add, ALU.mult).then_inc(s1_ready, 1)
                        dve.wait_ge(s1_ready, k + 1)
                        dve.sem_inc(bank_read[BANK_G[h]], 1)
                        b = BANK_U[h]
                        dve.wait_ge(bank_full[b], l * BANKS[b] + MIXED[b] + pr + 1)
                        V.scalar_tensor_tensor(hid[:, h, :], s1, 0.5, bank[b][:, :], ALU.mult, ALU.mult)\
                            .then_inc(bank_read[b], 1)
                        dve.wait_ge(bank_read[b], l * BANKS[b] + MIXED[b] + pr + 1)
                    for n in range(2):
                        b = BANK_D[n]
                        dve.wait_ge(bank_full[b], l * BANKS[b] + MIXED[b] + pr + 1)
                        V.tensor_tensor(osb[:, n * 512:(n + 1) * 512], bank[b][:, :], g2slot[:, n * 512:(n + 1) * 512],
                                        ALU.mult).then_inc(bank_read[b], 1)
                    for s in range(6):
                        n, t = s // 3, s % 3
                        b = (BANK_Y, BANK_T)[s % 2]
                        k = l * BANKS[b] + MIXED[b] + pr * PAIR[b] + s // 2 + (2 if b == BANK_T else 0)
                        dve.wait_ge(bank_full[b], k + 1)
                        xs = x[:, t, n * 512:(n + 1) * 512]
                        V.tensor_tensor(xs, xs, bank[b][:, :], ALU.add).then_inc(bank_read[b], 1)
                        dve.wait_ge(bank_read[b], k + 1)

        @block.tensor
        def _(pe):
            mm = nc.tensor.matmul
            turn_over = nc.tensor.transpose

            def begin(l, name):
                b, n = turn(l, name)
                if n:
                    pe.wait_ge(bank_read[b], n)
                return bank[b]

            def done(l, name, ins):
                ins.then_inc(bank_full[turn(l, name)[0]], 1)

            def arrived(l, u):
                n = UNIT_AT[u]
                pe.wait_ge(landed[n % RING], 16 * (l * LANDS[n % RING] + n // RING + 1))

            def mod(l, i):
                ps = begin(l, ("mod", i))
                for h in range(2):
                    arrived(l, ("mod", i, h))
                    w = unit_view(("mod", i, h))
                    for q in range(4):
                        ins = mm(ps[32 * q:32 * q + 32, :], cs[:, 4 * h + q, :], w[:, q, :], start=(h == 0), stop=(h == 1))
                    if h == 0:
                        ins.then_inc(first_half_used, 1)
                done(l, ("mod", i), ins)

            def mod_cols(l, k, i, j, last):
                wait_read(pe, l, ("mod", i))
                ps = bank[turn(l, ("modcol", k))[0]]
                for c in range(4):
                    ins = mm(ps[:, 8 * j + 2 * c:8 * j + 2 * c + 2], modrow[:, i % 2, c * P:(c + 1) * P], pair,
                             start=True, stop=True)
                if last:
                    done(l, ("modcol", k), ins)

            def norm_turn(l, name, k):
                pe.wait_ge(xn_ready, 6 * l + 3 * k + 3)
                for kb in range(KB):
                    ps = begin(l, (name, kb))
                    for t in range(T):
                        ins = turn_over(ps[:, t * P:(t + 1) * P], xn[:, t, kb * P:(kb + 1) * P], ident)
                    done(l, (name, kb), ins)

            def scores(l, i):
                sa, sbk = begin(l, ("sa", i)), begin(l, ("sb", i))
                if i < SH:
                    q, k = qT[:, i % 4, :], kTp[:, i // 4, :]
                else:
                    q, k = qmT[0:MQ, i - SH, :], kmT[0:MQ, i - SH, :]
                mm(sa[:, 0:P], q[:, 0:P], k[:, 0:P], start=True, stop=True)
                done(l, ("sa", i), mm(sa[:, P:512], q[:, P:2 * P], k[:, P:512], start=True, stop=True))
                done(l, ("sb", i), mm(sbk[:, 0:TOK], q[:, 2 * P:TOK], k[:, P:512], start=True, stop=True))

            def gate(l, b, j):
                ps = begin(l, ("gate", b, j))
                for h in range(2):
                    u = ("gate", (b, j // 4), h)
                    arrived(l, u)
                    w = unit_view(u)
                    for q in range(4):
                        ins = mm(ps[:, 0:TOK], w[:, q, (j % 4) * P:(j % 4 + 1) * P], hT[:, 4 * h + q, :],
                                 start=(h == 0 and q == 0), stop=(h == 1 and q == 3))
                    if h == 0 and j % 4 == 3:
                        ins.then_inc(first_half_used, 1)
                done(l, ("gate", b, j), ins)

            def branch(l, b, j):
                ps = begin(l, ("br", b, j))
                u = ("br", (b, j // 4), 0)
                arrived(l, u)
                if b == 1 and j == 0:
                    for i in range(4):
                        wait_read(pe, l, ("o", i))
                if b == 2 and j == 0:
                    for i in range(4, 8):
                        wait_read(pe, l, ("o", i))
                y = (yaT, ybT, yaT)[b]
                w = unit_view(u)
                for q in range(4):
                    ins = mm(ps[:, 0:TOK], w[:, q, (j % 4) * P:(j % 4 + 1) * P], y[:, q, :], start=(q == 0), stop=(q == 3))
                done(l, ("br", b, j), ins)

            def turn_probs(l, i):
                pe.wait_ge(prob_ready, 48 * l + 3 * i + 3)
                s = i % 2
                for name, at in (("x", range(4)), ("y", range(4, 7))):
                    ps = begin(l, (name, i))
                    for k, n in enumerate(at):
                        c = 0 if n == 0 else P + ((n - 1) % 2) * TOK + ((n - 1) // 2) * P
                        ins = turn_over(ps[:, k * P:(k + 1) * P], prob[:, s, c:c + P], ident)
                    done(l, (name, i), ins)

            def values(l, i):
                s = i % 2
                o = begin(l, ("o", i // 2)) if i % 2 == 0 else bank[turn(l, ("o", i // 2))[0]]
                wait_read(pe, l, ("x", i))
                wait_read(pe, l, ("y", i))
                r = SD * (i % 2)

                def v(t):
                    return vtok[:, t, SD * (i // 4):SD * (i // 4) + SD] if i < SH else vm[:, t, i - SH, :]
                mm(o[r:r + SD, 0:P], v(0), probT[:, s, 0, :], start=True, stop=True)
                for t in range(3):
                    ins = mm(o[r:r + SD, P:TOK], v(1 + t), probT[:, s, 1 + 2 * t:3 + 2 * t, :].rearrange("p a b -> p (a b)"),
                             start=(t == 0), stop=(t == 2))
                if i % 2:
                    done(l, ("o", i // 2), ins)

            pe.wait_ge(const_in, 48)
            pe.wait_ge(cond_ready, 1)
            for l in range(L):
                begin(l, ("modcol", 0))
                mod(l, 0)
                for i in range(1, 4):
                    mod(l, i)
                    mod_cols(l, 0, i - 1, i - 1, False)
                mod_cols(l, 0, 3, 3, True)
                norm_turn(l, "h1", 0)
                for kb in range(KB):
                    wait_read(pe, l, ("h1", kb))
                for s in range(3):
                    n = (512, 512, 416)[s]
                    for h in range(2):
                        arrived(l, ("seg", s, h))
                        w = unit_view(("seg", s, h))
                        for t in range(T):
                            ps = begin(l, ("seg", s, t)) if h == 0 else bank[turn(l, ("seg", s, t))[0]]
                            for q in range(4):
                                ins = mm(ps[:, 0:n], hT[:, 4 * h + q, t * P:(t + 1) * P], w[:, q, 0:n],
                                         start=(h == 0 and q == 0), stop=(h == 1 and q == 3))
                            if h == 0 and t == 2:
                                ins.then_inc(first_half_used, 1)
                            if h == 1:
                                done(l, ("seg", s, t), ins)
                for g in range(4):
                    ps = begin(l, ("u", g))
                    for h in range(2):
                        arrived(l, ("seg", 3, h))
                        w = unit_view(("seg", 3, h))
                        for q in range(4):
                            ins = mm(ps[:, 0:TOK], w[:, q, g * P:(g + 1) * P], hT[:, 4 * h + q, :],
                                     start=(h == 0 and q == 0), stop=(h == 1 and q == 3))
                        if h == 0 and g == 3:
                            ins.then_inc(first_half_used, 1)
                    done(l, ("u", g), ins)
                for t in range(T):
                    ps = begin(l, ("tq", t))
                    pe.wait_ge(qtok_ready, 3 * l + t + 1)
                    for b in range(4):
                        ins = turn_over(ps[:, b * P:(b + 1) * P], qtok[:, t, b * P:(b + 1) * P], ident)
                    done(l, ("tq", t), ins)
                for t in range(T):
                    ps = begin(l, ("tkc", t))
                    pe.wait_ge(ktok_ready, 3 * l + t + 1)
                    turn_over(ps[:, 0:P], ktok[:, t, :], ident)
                    pe.wait_ge(qctok_ready, 3 * l + t + 1)
                    for b in range(3):
                        ins = turn_over(ps[:, (1 + b) * P:(2 + b) * P], qctok[:, t, b * P:(b + 1) * P], ident)
                    done(l, ("tkc", t), ins)
                for k, tiles in enumerate(((0, 1), (2,))):
                    ps = begin(l, ("tkv", k))
                    for n, t in enumerate(tiles):
                        pe.wait_ge(ckvtok_ready, 3 * l + t + 1)
                        for b in range(2):
                            ins = turn_over(ps[:, (2 * n + b) * P:(2 * n + b + 1) * P], ckvtok[:, t, b * P:(b + 1) * P], ident)
                    done(l, ("tkv", k), ins)
                for t in range(T):
                    wait_read(pe, l, ("tkc", t))
                for h in range(2):
                    arrived(l, ("wq", h, 0))
                    w = ring[:, slot_of(("wq", h, 0)), 0:3 * QR].rearrange("p (k n) -> p k n", n=QR)
                    for t in range(T):
                        ps = begin(l, ("wq", h, t))
                        for k in range(3):
                            ins = mm(ps[:, 0:QR], qcT[:, k, t * P:(t + 1) * P], w[:, k, :], start=(k == 0), stop=(k == 2))
                        done(l, ("wq", h, t), ins)
                for g in range(4):
                    ps = begin(l, ("pool", g))
                    pe.wait_ge(pool_ready, 8 * l + 2 * g + 2)
                    done(l, ("pool", g), mm(ps[:, 0:TOK], poolw[:, g, :], yaT[:, g, :], start=True, stop=True))
                for k in range(2):
                    wait_read(pe, l, ("tkv", k))
                arrived(l, ("wkv", 0, 0))
                w = ring[:, slot_of(("wkv", 0, 0)), :].rearrange("p (k n) -> p k n", n=D)

                def turn_heads(name, t, n):
                    pe.wait_ge(tok_ready, 7 * l + n + 1)
                    v = tok[:, n % 2, :].rearrange("p (h d) -> p h d", d=MQ)
                    for h in range(2):
                        ps = begin(l, (name, t, h))
                        for k in range(4):
                            ins = turn_over(ps[0:MQ, k * P:(k + 1) * P], v[:, 4 * h + k, :], ident)
                        done(l, (name, t, h), ins)
                for t in range(4):
                    for h in range(2):
                        ps = begin(l, ("wkv", t, h))
                        for k in range(2):
                            ins = mm(ps[:, :], ckvT[:, k, t * P:(t + 1) * P], w[:, k, h * 512:(h + 1) * 512],
                                     start=(k == 0), stop=(k == 1))
                        done(l, ("wkv", t, h), ins)
                    if t < 3:
                        turn_heads("tqm", t, t)
                for t in range(4):
                    turn_heads("tkm", t, 3 + t)
                for t in range(T):
                    wait_read(pe, l, ("tq", t))
                scores(l, 0)
                for g in range(4):
                    wait_read(pe, l, ("pool", g))
                for i in range(SH + MH):
                    if i == 7:
                        for t in range(3):
                            for h in range(2):
                                wait_read(pe, l, ("tqm", t, h))
                        for t in range(4):
                            for h in range(2):
                                wait_read(pe, l, ("tkm", t, h))
                    if i < 15:
                        scores(l, i + 1)
                    gate(l, i // 8, i % 8)
                    turn_probs(l, i)
                    branch(l, i // 8, i % 8)
                    values(l, i)
                for i in (4, 5):
                    mod(l, i)
                for i in (4, 5):
                    wait_read(pe, l, ("mod", i))
                    for v in range(2):
                        ps = begin(l, ("modb", i, v))
                        done(l, ("modb", i, v), mm(ps[:, :], pick[v], modrow[:, i % 2, :], start=True, stop=True))
                for j in range(KB):
                    gate(l, 2, j)
                    branch(l, 2, j)
                pe.wait_ge(merged_ready, 24 * (l + 1))
                for n in range(2):
                    for h in range(2):
                        arrived(l, ("wo", n, h))
                        w = unit_view(("wo", n, h))
                        for t in range(T):
                            ps = begin(l, ("wo", n, t)) if h == 0 else bank[turn(l, ("wo", n, t))[0]]
                            for q in range(4):
                                ins = mm(ps[:, :], merged[:, 4 * h + q, t * P:(t + 1) * P], w[:, q, :],
                                         start=(h == 0 and q == 0), stop=(h == 1 and q == 3))
                            if h == 0 and t == 2:
                                ins.then_inc(first_half_used, 1)
                            if h == 1:
                                done(l, ("wo", n, t), ins)
                begin(l, ("modcol", 1))
                mod(l, 6)
                for i in range(7, 10):
                    mod(l, i)
                    mod_cols(l, 1, i - 1, i - 7, False)
                mod(l, 10)
                mod_cols(l, 1, 9, 3, True)
                mod(l, 11)
                for i in (10, 11):
                    wait_read(pe, l, ("mod", i))
                    ps = begin(l, ("modb", i, 0))
                    done(l, ("modb", i, 0), mm(ps[:, :], pickslot, modrow[:, i % 2, :], start=True, stop=True))
                norm_turn(l, "h2", 1)
                for kb in range(KB):
                    wait_read(pe, l, ("h2", kb))
                pe.wait_ge(layer_in, 16 * 9 * (l + 1))
                ps = begin(l, ("route", 0))
                for t in range(T):
                    for kb in range(KB):
                        ins = mm(ps[:, t * NE:(t + 1) * NE], hT[:, kb, t * P:(t + 1) * P], wrout[:, kb, :],
                                 start=(kb == 0), stop=(kb == KB - 1))
                done(l, ("route", 0), ins)
                ps = begin(l, ("afft", 0))
                pe.wait_ge(aff_ready, l + 1)
                for t in range(T):
                    ins = turn_over(ps[0:NE, t * P:(t + 1) * P], aff[:, t, :], ident)
                done(l, ("afft", 0), ins)
                ps = begin(l, ("get", 0))
                pe.wait_ge(ge_ready, l + 1)
                for t in range(T):
                    for k in range(2):
                        ins = turn_over(ps[:, (2 * t + k) * NE:(2 * t + k + 1) * NE],
                                        ge[0:NE, k * TOK + t * P:k * TOK + (t + 1) * P], ident[0:NE, 0:NE])
                done(l, ("get", 0), ins)
                wait_read(pe, l, ("get", 0))
                ps = begin(l, ("cum", 0))
                for t, before, all_ in ((0, (), (0,)), (1, (), (1, 2)), (2, (1,), (1, 2))):
                    c = 2 * NE * t
                    mm(ps[:, c:c + 2 * NE], tri, get[:, t, :], start=True, stop=False)
                    for k in before:
                        mm(ps[:, c:c + 2 * NE], ones, get[:, k, :], start=False, stop=False)
                    for k in all_:
                        ins = mm(ps[:, c + NE:c + 2 * NE], ones, get[:, k, 0:NE], start=False, stop=(k == all_[-1]))
                done(l, ("cum", 0), ins)
                pe.wait_ge(sel_ready, 3 * (l + 1))
                for kb in range(KB):
                    for h in range(2):
                        ps = begin(l, ("gather", kb, h))
                        v = ps[:, 0:8 * USED].rearrange("p (e s) -> p e s", s=USED)

                        def chosen(t, lo, hi):
                            return sel[:, t, :].rearrange("p (e s) -> p e s", s=SLOTS)[:, 8 * h:8 * h + 8, lo:hi]
                        mm(v[:, :, 0:CP], xn[:, 0, kb * P:(kb + 1) * P], chosen(0, 0, CP), start=True, stop=True)
                        for t in (1, 2):
                            ins = mm(v[:, :, CP:USED], xn[:, t, kb * P:(kb + 1) * P], chosen(t, CP, USED),
                                     start=(t == 1), stop=(t == 2))
                        done(l, ("gather", kb, h), ins)
                pe.wait_ge(selv_ready, 3 * (l + 1))
                for pr in range(NP):
                    ps = begin(l, ("selt", pr))
                    for t in range(T):
                        ins = turn_over(ps[:, t * P:(t + 1) * P], sel[:, t, pr * P:(pr + 1) * P], ident)
                    done(l, ("selt", pr), ins)
                with pe.Fori(0, NP) as pr:
                    def begin_pair(b, k):
                        pe.wait_ge(bank_read[b], l * BANKS[b] + MIXED[b] + pr * PAIR[b] + k)

                    def project(g, b, lhs):
                        begin_pair(b, 0)
                        for h in range(2):
                            for e in range(2):
                                s = (4 * g + 2 * h + e) % RING
                                pe.wait_ge(landed[s], 16 * (l * LANDS[s] + LANDED[s] + pr * 3 + (4 * g + 2 * h + e) // RING + 1))
                            for q in range(4):
                                for e in range(2):
                                    w = ring[:, (4 * g + 2 * h + e) % RING, :].rearrange("p (k n) -> p k n", n=512)
                                    ins = mm(bank[b][64 * e:64 * e + 64, :], lhs(e, 4 * h + q), w[:, q, :],
                                             start=(h == 0 and q == 0), stop=(h == 1 and q == 3))
                                    if h == 0 and q == 3:
                                        ins.then_inc(first_half_used, 1)
                        ins.then_inc(bank_full[b], 1)

                    pe.wait_ge(xcur_ready, l * 2 * NP + pr * 2 + 2)
                    for h in range(2):
                        project(2 * h, BANK_G[h], lambda e, kb: xcur[:, e, kb, :])
                        project(2 * h + 1, BANK_U[h], lambda e, kb: xcur[:, e, kb, :])
                    for h in range(2):
                        begin_pair(BANK_T, h)
                        b = BANK_U[h]
                        pe.wait_ge(bank_read[b], l * BANKS[b] + MIXED[b] + pr + 1)
                        for k in range(4):
                            ins = turn_over(bank[BANK_T][:, k * P:(k + 1) * P], hid[:, h, k * P:(k + 1) * P], ident)
                        ins.then_inc(bank_full[BANK_T], 1)
                    begin_pair(BANK_T, 2)
                    for n in range(2):
                        project(4 + n, BANK_D[n], lambda e, kb: hidT[:, kb, 64 * e:64 * e + 64])
                    pe.wait_ge(selcur_ready, l * NP + pr + 1)
                    for s in range(6):
                        n, t = s // 3, s % 3
                        if t == 0:
                            b = BANK_D[n]
                            pe.wait_ge(bank_read[b], l * BANKS[b] + MIXED[b] + pr + 1)
                        b = (BANK_Y, BANK_T)[s % 2]
                        begin_pair(b, s // 2 + (2 if b == BANK_T else 0))
                        mm(bank[b][:, :], selcur[:, t * P:(t + 1) * P], osb[:, n * 512:(n + 1) * 512],
                           start=True, stop=True).then_inc(bank_full[b], 1)


INPUTS = ["x_prompt", "x_sample", "w_mod", "b_mod", "w_in", "pool_w", "w_q_b", "w_kv_b", "w_br_a", "w_br_b", "w_br_c",
          "w_out", "w_router", "w_gate", "w_up", "w_down"]
OUTPUTS = [(1, P, D), (1, 2 * P, D), (1, L, P, P), (1, L, P, P), (1, L, P, KVR), (1, L, P, ROPE)]


def kernel(**inputs):
    import concourse.bacc as _bacc
    from concourse.bass_utils import run_bass_kernel_spmd as _run

    v = {k: np.asarray(a) for k, a in inputs.items()}
    arrays = {n: v[n] for n in INPUTS}

    def columns(a, n):
        return a.reshape(L, n, P).transpose(2, 0, 1)
    arrays["cols"] = np.concatenate([columns(v["b_mod"], 48), columns(v["norm1_g"], KB), columns(v["norm2_g"], KB),
                                     columns(v["pool_scale"], 4)], axis=2)
    arrays["rows"] = np.concatenate([v["swa_q_g"], v["swa_k_g"], v["mla_q_norm_g"], v["mla_kv_norm_g"], v["mla_q_g"],
                                     v["mla_k_g"], v["sink"]], axis=1)
    cond = np.zeros((P, KB, 32), np.float32)
    cond[:, :, 0] = v["c_ctx"].reshape(KB, P).T
    cond[:, :, 1] = v["c"][0].reshape(KB, P).T
    arrays["condT"] = cond
    arrays["ctx_kT"] = v["cache_swa_k"][0].reshape(L, P, P).transpose(0, 2, 1)
    arrays["ctx_v"] = v["cache_swa_v"][0].reshape(L, P, P)
    arrays["ctx_ckvT"] = v["cache_mla_ckv"][0].transpose(0, 2, 1)
    arrays["ctx_kr"] = v["cache_mla_krope"][0]
    arrays["const"] = const_table()
    arrays["counts"] = count_table()

    nc = _bacc.Bacc("TRN2", target_bir_lowering=False, num_devices=1)
    arrays = {n: np.ascontiguousarray(a) for n, a in arrays.items()}
    aps = {n: nc.dram_tensor(f"in_{n}", a.shape, F32, kind="ExternalInput").ap() for n, a in arrays.items()}
    outs = [nc.dram_tensor(f"out_{i}", s, F32, kind="ExternalOutput").ap() for i, s in enumerate(OUTPUTS)]
    hybrid_step(nc, aps, outs)
    r = _run(nc, [{f"in_{n}": a for n, a in arrays.items()}], core_ids=[0]).results[0]
    got = [r[f"out_{i}"] for i in range(6)]
    got[2] = got[2].reshape(1, L, P, 2, SD)
    got[3] = got[3].reshape(1, L, P, 2, SD)
    return tuple(got)
```

```python
from contextlib import ExitStack

import numpy as np

import concourse.bass as bass
from concourse import mybir

F32 = mybir.dt.float32
ALU = mybir.AluOpType
ACT = mybir.ActivationFunctionType
AX = mybir.AxisListType.X

P = 128
D = 1024
KB = D // P
L = 2
T = 3
TOK = T * P
EPS = 1e-6
SH, SD = 8, 64
MH, MQ, NOPE, ROPE, MV = 8, 96, 64, 32, 64
QR, KVR = 384, 256
NE = 16
CP, CS = 16, 32
SLOTS = 64
USED = CP + CS
NP = NE // 2
UNIT = 2048
RING = 8
RINGX = 12
NEG = -1e30
BIG = 4096.0

COL_B, COL_N1, COL_N2, COL_PS, NCOL = 0, 48, 56, 64, 68
ROW_QG, ROW_KG, ROW_QCG, ROW_KVG, ROW_MQG, ROW_MKG, ROW_SINK, NROW = 0, 64, 128, 512, 768, 864, 960, 968
_sizes = [("ident", P), ("tri", P), ("ones", P), ("pick0", P), ("pick1", P), ("pickslot", P), ("pair", 2), ("fold", NE),
          ("slotno", 2 * SLOTS), ("band", 2 * P), ("ropes", 2 * 2 * SD), ("ropem", 2 * 2 * ROPE)]
CONST = {}
_at = 0
for _n, _s in _sizes:
    CONST[_n] = (_at, _at + _s)
    _at += _s
NCONST = _at


def const_table():
    t = np.zeros((P, NCONST), np.float32)
    r = np.arange(P)

    def put(name, a):
        lo, hi = CONST[name]
        t[:, lo:hi] = a.reshape(P, hi - lo)
    put("ident", np.eye(P))
    put("tri", (r[:, None] < r[None, :]).astype(np.float32))
    put("ones", np.ones((P, P)))
    put("pick0", np.repeat((r % 32 == 0)[:, None], P, 1))
    put("pick1", np.repeat((r % 32 == 1)[:, None], P, 1))
    s = r % SLOTS
    stream = np.where(s < CP, 0, np.where(s < USED, 1, -1))
    put("pickslot", (r[:, None] % 32 == stream[None, :]))
    put("pair", np.stack([r % 32 == 0, r % 32 == 1], 1))
    put("fold", (r[:, None] % 32 == np.arange(NE)[None, :]))
    k = np.arange(SLOTS)
    put("slotno", np.repeat(np.stack([np.where(k < CP, k, -1), np.where((k >= CP) & (k < USED), k - CP, -1)])[None], P, 0))
    put("band", np.stack([np.where(r[None, :] <= r[:, None], 0, NEG), np.where(r[:, None] <= r[None, :], 0, NEG)], 1))

    def rope(width):
        q = width // 4
        f = (np.float32(10000.0) ** (-np.arange(q, dtype=np.float32) / np.float32(q))).astype(np.float32)
        pos = np.arange(2 * P)
        out = np.zeros((P, 2, 2, 2, 2, q), np.float32)
        for axis, where in enumerate((pos // 64, pos % 64)):
            ang = (where.astype(np.float32)[:, None] * f[None, :]).astype(np.float32).astype(np.float64)
            c, s = (g(ang).reshape(2, P, q).transpose(1, 0, 2) for g in (np.cos, np.sin))
            out[:, :, 0, axis, 0] = out[:, :, 0, axis, 1] = c
            out[:, :, 1, axis, 0], out[:, :, 1, axis, 1] = -s, s
        return out
    put("ropes", rope(SD))
    put("ropem", rope(ROPE))
    return t


PADW = 416
PSEG = ((8, 0, P), (8 + P + 8 + 8, P, 2 * P))


def count_table():
    out = np.zeros((4, TOK), np.float32)
    for g in range(4):
        w = 2 << g
        for _, t0, n in PSEG:
            t = np.arange(n)
            out[g, t0:t0 + n] = 1.0 / (np.clip(t + w // 2, 0, n) - np.clip(t - w // 2, 0, n))
    return out.reshape(1, 4 * TOK)


def plan_banks():
    uses = []

    def use(name, bank):
        uses.append((name, bank))
    for i in range(4):
        use(("mod", i), i % 2)
    use(("modcol", 0), 2)
    for kb in range(KB):
        use(("h1", kb), 4 + kb % 4)
    for s in range(3):
        for t in range(T):
            use(("seg", s, t), (3 * s + t) % 8)
    for g in range(4):
        use(("u", g), 1 + g)
    use(("mod", 6), 1)
    for t in range(T):
        use(("tq", t), 5 + t)
    for t in range(T):
        use(("tkc", t), t)
    for t in range(2):
        use(("tkv", t), 3 + t)
    use(("mod", 7), 7)
    for h in range(2):
        for t in range(T):
            use(("wq", h, t), 1 + 3 * h + t)
    for g in range(4):
        use(("pool", g), (7, 0)[g % 2])
    for i in (8, 9):
        use(("mod", i), (7, 0)[i % 2])
    for t in range(4):
        for h in range(2):
            use(("wkv", t, h), (1, 3, 5, 1)[t] + h)
        if t < 3:
            for h in range(2):
                use(("tqm", t, h), (7, 0)[h])
    use(("modcol", 1), 7)
    for t in range(4):
        for h in range(2):
            use(("tkm", t, h), (3 + 2 * t + h) % 8 if t < 3 else 1 + h)
    for i in range(SH + MH):
        use(("sa", i), 2 * (i % 2))
        use(("sb", i), 2 * (i % 2) + 1)
        use(("x", i), 4)
        use(("y", i), 5)
        if i % 2 == 0:
            use(("o", i // 2), 6)
        use(("gate", i // 8, i % 8), 7)
        use(("br", i // 8, i % 8), 7)
    for i in (4, 5):
        use(("mod", i), i - 1)
    for i in (4, 5):
        for v in range(2):
            use(("modb", i, v), 5 + v)
    for j in range(KB):
        use(("gate", 2, j), (7, 0)[j % 2])
        use(("br", 2, j), (1, 2)[j % 2])
    for n in range(2):
        for t in range(T):
            use(("wo", n, t), 3 * n + t)
    for i in (10, 11):
        use(("mod", i), 6 + i % 2)
    for i in (10, 11):
        use(("modb", i, 0), i - 9)
    for kb in range(KB):
        use(("h2", kb), 2 + kb % 4)
    use(("rpart", 0), 6)
    use(("route", 0), 0)
    use(("afft", 0), 7)
    use(("get", 0), 6)
    use(("cum", 0), 1)
    count, where = [0] * 8, {}
    for name, bank in uses:
        where[name] = (bank, count[bank])
        count[bank] += 1
    return where, count


WHERE, MIXED = plan_banks()
BANK_G, BANK_U, BANK_D, BANK_T, BANK_Y = (0, 2), (1, 3), (5, 6), 4, 7
PROJECT = {0: 1, 1: 1, 2: 0, 3: 0, 5: 0, 6: 0}
PAIR = [2, 2, 1, 1, 5, 1, 1, 4]
BANKS = [m + NP * k for m, k in zip(MIXED, PAIR)]


def plan_units():
    units = []
    for i in range(4):
        units += [("mod", i, 0), ("mod", i, 1)]
    for s in range(4):
        units += [("seg", s, 0), ("seg", s, 1)]
    for i in (6, 7):
        units += [("mod", i, 0), ("mod", i, 1)]
    units += [("wq", 0, 0), ("wq", 1, 0)]
    for i in (8, 9):
        units += [("mod", i, 0), ("mod", i, 1)]
    units += [("wkv", 0, 0)]
    for b in range(3):
        if b == 2:
            for i in (4, 5):
                units += [("mod", i, 0), ("mod", i, 1)]
        for h in range(2):
            units += [("gate", (b, h), 0), ("gate", (b, h), 1), ("br", (b, h), 0)]
    for n in range(2):
        units += [("wo", n, 0), ("wo", n, 1)]
    for i in (10, 11):
        units += [("mod", i, 0), ("mod", i, 1)]
    return units


UNITS = plan_units()
NU = len(UNITS)
UNIT_AT = {u: n for n, u in enumerate(UNITS)}
LANDED = [sum(n % RING == s for n in range(NU)) if s < RING else 0 for s in range(RINGX)]
LANDS = [c + 24 // RINGX * NP for c in LANDED]
FIRSTS = [u for u in UNITS if u[2] == 0 and u[0] in ("mod", "seg", "gate", "wo")]
FIRST_AT = {u: n for n, u in enumerate(FIRSTS)}
HALVES = len(FIRSTS) + 12 * NP


def last_group(u):
    kind, i, _ = u
    if kind == "mod":
        return ("mod", i)
    if kind == "seg":
        return ("seg", i, 2) if i < 3 else ("u", 3)
    if kind == "wq":
        return ("wq", i, 2)
    if kind == "wkv":
        return ("wkv", 3, 1)
    if kind in ("gate", "br"):
        return (kind, i[0], 4 * i[1] + 3)
    return ("wo", i, 2)


def hybrid_step(nc, a, outs):
    with ExitStack() as ctx:
        def sb(name, shape):
            return ctx.enter_context(nc.sbuf_tensor(name, shape, F32))

        def sem(name):
            return ctx.enter_context(nc.semaphore(name))

        x = sb("x", [P, T, D])
        hT = sb("hT", [P, KB, TOK])
        xn = sb("xn", [P, T, D])
        merged = xn[:, :, :].rearrange("p t d -> p (t d)").rearrange("p (k n) -> p k n", n=TOK)
        ring = sb("ring", [P, RING, UNIT])
        kTp = sb("kTp", [P, 2, 512])
        xcur = sb("xcur", [P, 2, KB, SLOTS])
        cols = sb("cols", [P, L, NCOL])
        rows = sb("rows", [P, NROW])
        const = sb("const", [P, NCONST])
        cs = sb("cs", [P, KB, 32])
        modrow = sb("modrow", [P, 2, 512])
        shift = [sb(f"shift{k}", [P, KB, 2]) for k in range(2)]
        amp = [sb(f"amp{k}", [P, KB, 2]) for k in range(2)]
        g2slot = sb("g2slot", [P, D])
        wrout = sb("wrout", [P, KB, 32])
        kr = sb("kr", [P, 4, ROPE])
        krg = sb("krg", [P, 4, ROPE])
        sskr = sb("sskr", [P, 4])
        ss = sb("ss", [P, 98])
        var = sb("var", [P, 98])
        rstd = sb("rstd", [P, 98])
        mhalf = sb("mhalf", [P, 8])
        negsink = sb("negsink", [P, SH])
        mx = sb("mx", [P, 2, 3])
        negm = sb("negm", [P, 2, 3])
        rsum = sb("rsum", [P, 2, 3])
        esink = sb("esink", [P, 2, 3])
        rinv = sb("rinv", [P, 2, 3])

        M = sb("M", [P, 19584])

        def view(at, *dims):
            n = int(np.prod(dims))
            v = M[:, at:at + n]
            if len(dims) == 2:
                v = v.rearrange("p (a b) -> p a b", b=dims[1])
            if len(dims) == 3:
                v = v.rearrange("p (a b c) -> p a b c", b=dims[1], c=dims[2])
            return v
        qmT = view(0, MH, TOK)
        upad = view(0, 4, PADW)
        win = view(4 * PADW, 2, PADW)
        kmT = view(3072, MH, 512)
        qtok = view(3072, T, 512)
        ktok = view(4608, T, P)
        qctok = view(4992, T, QR)
        ckvtok = view(6144, T, KVR)
        g1b = view(3072, 2, D)
        gb = view(5120, D)
        vm = view(7168, 4, MH, MV)
        inv = view(7168, 4, TOK)
        poolw = view(8704, 4, P)
        vtok = view(9216, 4, P)
        yaT = view(9728, 4, TOK)
        ybT = view(11264, 4, TOK)
        ropea = view(11264, 768)
        ropeb = view(12032, 768)
        qT = view(12800, 4, TOK)
        junk = view(14336, D)
        qcT = view(14336, 3, TOK)
        ckvT = view(15488, 2, 512)
        sqb = view(16512, 2, 768)
        tok = view(18048, 2, 768)
        cond = view(18048, KB, 32)
        prob = view(14336, 2, 896)
        probT = view(16128, 2, 7, P)
        tanh_g = view(17920, 2, TOK)
        gated = view(18688, TOK)
        wtmp = view(15360, 2, 512)
        more_ring = view(0, RINGX - RING, UNIT)
        gsel = view(8192, T, P)
        vsel = view(8576, T, P)
        sel = view(9216, T, NE * SLOTS)
        selT = view(12288, TOK)
        th = (view(12672, 512), view(18672, 512))
        s1 = view(13184, 512)
        hid = view(13696, 2, 512)
        hidT = view(14720, KB, P)
        osb = view(15744, D)
        logit = view(17792, T, NE)
        aff = view(17840, T, NE)
        small = view(17888, 16)
        affT = view(17904, TOK)
        work = view(18288, TOK)
        ge = view(18672, 2 * TOK)
        get = view(19440, T, 2 * NE)
        top8 = view(19536, 8)
        rpart = view(18288, TOK)
        sl1 = view(17904, T, NE)
        sl2 = view(17952, T, NE)

        bank = [ctx.enter_context(nc.psum_tensor(f"bank{b}", [P, 512], F32)) for b in range(8)]

        def cst_(name, *dims):
            lo, hi = CONST[name]
            v = const[:, lo:hi]
            if len(dims) == 2:
                v = v.rearrange("p (a b) -> p a b", b=dims[1])
            if len(dims) == 3:
                v = v.rearrange("p (a b c) -> p a b c", b=dims[1], c=dims[2])
            return v
        ident, tri, ones = cst_("ident"), cst_("tri"), cst_("ones")
        pick = (cst_("pick0"), cst_("pick1"))
        pickslot, pair = cst_("pickslot"), cst_("pair")
        fold = cst_("fold")
        slotno = cst_("slotno", 2, SLOTS)
        band = cst_("band", 2, P)
        ropes = cst_("ropes", 2, 2, SD)
        ropem = cst_("ropem", 2, 2, ROPE)

        bank_full = [sem(f"bank_full{b}") for b in range(8)]
        bank_read = [sem(f"bank_read{b}") for b in range(8)]
        landed = [sem(f"landed{s}") for s in range(RINGX)]
        first_half_used = sem("first_half_used")
        x_in = sem("x_in")
        const_in = sem("const_in")
        layer_in = sem("layer_in")
        gate_row_in = sem("gate_row_in")
        out_done = sem("out_done")
        cache_out = sem("cache_out")
        pads_zero = sem("pads_zero")
        cond_tanh = sem("cond_tanh")
        cond_ready = sem("cond_ready")
        act_step = sem("act_step")
        dve_step = sem("dve_step")
        pool_step = sem("pool_step")
        xss_ready = sem("xss_ready")
        var_ready = sem("var_ready")
        rstd_ready = sem("rstd_ready")
        xn_ready = sem("xn_ready")
        cols_ready = sem("cols_ready")
        sq_ready = sem("sq_ready")
        sq_used = sem("sq_used")
        cseg_read = sem("cseg_read")
        dseg_read = sem("dseg_read")
        v_read = sem("v_read")
        qtok_ready = sem("qtok_ready")
        ktok_ready = sem("ktok_ready")
        qctok_ready = sem("qctok_ready")
        ckvtok_ready = sem("ckvtok_ready")
        tok_ready = sem("tok_ready")
        pool_ready = sem("pool_ready")
        negm_ready = sem("negm_ready")
        sink_ready = sem("sink_ready")
        prob_ready = sem("prob_ready")
        merged_ready = sem("merged_ready")
        x_mixed = sem("x_mixed")
        exp_in_ready = sem("exp_in_ready")
        exp_ready = sem("exp_ready")
        aff_ready = sem("aff_ready")
        ge_ready = sem("ge_ready")
        sel_ready = sem("sel_ready")
        gsel_ready = sem("gsel_ready")
        vsel_ready = sem("vsel_ready")
        xcur_ready = sem("xcur_ready")
        th_ready = sem("th_ready")

        block = ctx.enter_context(nc.Block())

        def turn(l, name):
            b, n = WHERE[name]
            return b, l * BANKS[b] + n

        def wait_full(e, l, name):
            b, n = turn(l, name)
            e.wait_ge(bank_full[b], n + 1)
            return bank[b]

        def wait_read(e, l, name):
            b, n = turn(l, name)
            e.wait_ge(bank_read[b], n + 1)

        def read(l, name, ins):
            b, _ = turn(l, name)
            ins.then_inc(bank_read[b], 1)

        def in_pair(l, b, pr, k):
            return l * BANKS[b] + MIXED[b] + pr * PAIR[b] + k

        def for_pairs(e, body):
            with e.Fori(0, NP - 1) as pr:
                body(pr, True)
            body(NP - 1, False)

        def x_final(e, l):
            for b in (BANK_T, BANK_Y):
                e.wait_ge(bank_read[b], (l + 1) * BANKS[b])

        def steps(e, s):
            count = [0]

            def step(ins):
                count[0] += 1
                ins.then_inc(s, 1)
                e.wait_ge(s, count[0])
            return step

        def unit_source(l, u):
            kind, i, h = u
            if kind == "mod":
                w = a["w_mod"][l, h * 512:(h + 1) * 512, i * 512:(i + 1) * 512]
            elif kind == "seg":
                c0, n = ((512, 512), (1024, 512), (1536, 416), (0, 512))[i]
                w = a["w_in"][l, h * 512:(h + 1) * 512, c0:c0 + n]
            elif kind == "wq":
                w = a["w_q_b"][l, :, i * QR:(i + 1) * QR]
            elif kind == "wkv":
                w = a["w_kv_b"][l]
            elif kind == "gate":
                c0 = 1952 + i[0] * D + i[1] * 512
                w = a["w_in"][l, h * 512:(h + 1) * 512, c0:c0 + 512]
            elif kind == "br":
                w = a[("w_br_a", "w_br_b", "w_br_c")[i[0]]][l, :, i[1] * 512:(i[1] + 1) * 512]
            else:
                w = a["w_out"][l, h * 512:(h + 1) * 512, i * 512:(i + 1) * 512]
            return w.rearrange("(k p) n -> p k n", p=P)

        def slot_of(u):
            return UNIT_AT[u] % RING

        def expert_slot(s):
            at = ring[:, s, :] if s < RING else more_ring[:, s - RING, :]
            return at.rearrange("p (k n) -> p k n", n=512)

        def row_of(i):
            return g2slot[:, (i - 8) * 512:(i - 7) * 512] if i in (8, 9) else modrow[:, i % 2, :]

        def unit_view(u, width=512):
            return ring[:, slot_of(u), :].rearrange("p (k n) -> p k n", n=width)

        @block.sync
        def _(sp):
            sp.dma_start(cond, a["condT"]).then_inc(const_in, 16)
            sp.dma_start(const[:, :], a["const"]).then_inc(const_in, 16)
            sp.dma_start(cols[:, :, :], a["cols"]).then_inc(const_in, 16)
            sp.dma_start(x[:, 0, :], a["x_prompt"][0]).then_inc(x_in, 16)
            sp.dma_start(x[:, 1:3, :], a["x_sample"][0].rearrange("(t p) d -> p t d", p=P)).then_inc(x_in, 16)

            def wait_pair(l, pr, j):
                g, r = j // 4, j % 4
                if r < 2:
                    sp.wait_ge(first_half_used, l * HALVES + len(FIRSTS) + pr * 12 + 2 * g + r + 1)
                else:
                    b = (0, 1, 2, 3, 5, 6)[g]
                    sp.wait_ge(bank_full[b], in_pair(l, b, pr, PROJECT[b]) + 1)

            def wait_mixing(l, u):
                if u in FIRST_AT:
                    sp.wait_ge(first_half_used, l * HALVES + FIRST_AT[u] + 1)
                else:
                    wait_full(sp, l, last_group(u))

            def load_pair(l, pr, first):
                for j in range(24):
                    s = j % RINGX
                    if j >= RINGX:
                        wait_pair(l, pr, j - RINGX)
                    elif not first:
                        wait_pair(l, pr - 1, j + 24 - RINGX)
                    elif s >= RING:
                        sp.wait_ge(x_mixed, 3 * (l + 1))
                    else:
                        before = [n for n in range(NU) if n % RING == s][-1]
                        wait_mixing(l, UNITS[before])
                    g, h, e = j // 4, (j % 4) // 2, j % 2
                    w = (a["w_gate"], a["w_up"], a["w_gate"], a["w_up"], a["w_down"], a["w_down"])[g]
                    c = (0, 0, 1, 1, 0, 1)[g]
                    src = w[l, 2 * pr + e, h * 512:(h + 1) * 512, c * 512:(c + 1) * 512]
                    sp.dma_start(expert_slot(s),
                                 src.rearrange("(k p) n -> p k n", p=P)).then_inc(landed[s], 16)

            for l in range(L):
                for n, u in enumerate(UNITS):
                    if n >= RING:
                        wait_mixing(l, UNITS[n - RING])
                    elif l > 0:
                        wait_pair(l - 1, NP - 1, n + 24 - RINGX)
                    src = unit_source(l, u)
                    k, width = src.shape[1], src.shape[2]
                    sp.dma_start(ring[:, n % RING, 0:k * width].rearrange("p (k n) -> p k n", n=width) if width != 416
                                 else ring[:, n % RING, :].rearrange("p (k n) -> p k n", n=512)[:, :, 0:416],
                                 src).then_inc(landed[n % RING], 16)
                load_pair(l, 0, True)
                with sp.Fori(1, NP) as pr:
                    load_pair(l, pr, False)
            x_final(sp, L - 1)
            sp.dma_start(outs[0][0], x[:, 0, :]).then_inc(out_done, 16)
            sp.dma_start(outs[1][0].rearrange("(t p) d -> p t d", p=P), x[:, 1:3, :]).then_inc(out_done, 16)
            sp.wait_ge(out_done, 32)
            sp.wait_ge(cache_out, 64 * L)

        @block.gpsimd
        def _(pool):
            step = steps(pool, pool_step)
            step(nc.gpsimd.memset(mhalf[:, :], -0.5))
            nc.gpsimd.memset(kTp[:, :, :], 0.0).then_inc(pads_zero, 1)
            nc.gpsimd.memset(xcur[:, :, :, :], 0.0).then_inc(pads_zero, 1)
            nc.gpsimd.memset(wrout[:, :, :], 0.0).then_inc(pads_zero, 1)
            events = [0]

            def power(c0, n):
                events[0] += 1
                pool.wait_ge(var_ready, events[0])
                nc.gpsimd.tensor_tensor(rstd[:, c0:c0 + n], var[:, c0:c0 + n], mhalf[:, 0:n], ALU.pow)\
                    .then_inc(rstd_ready, 1)

            for l in range(L):
                if l == 0:
                    pool.wait_ge(pads_zero, 3)
                else:
                    x_final(pool, l - 1)
                loads = [
                    (rows[:, :], a["rows"][l].partition_broadcast(P)),
                    (poolw, a["pool_w"][l].rearrange("g c d -> c g d")),
                    (inv.rearrange("p g t -> p (g t)"), a["counts"][0].partition_broadcast(P)),
                    (wrout[:, :, 0:NE], a["w_router"][l].rearrange("(k p) e -> p k e", p=P)),
                    (kTp[0:SD, 0, TOK:512], a["ctx_kT"][l, 0:SD, :]),
                    (kTp[SD:P, 1, TOK:512], a["ctx_kT"][l, SD:P, :]),
                    (vtok[:, 3, :], a["ctx_v"][l]),
                    (ckvT[:, :, TOK:512], a["ctx_ckvT"][l].rearrange("(k p) t -> p k t", p=P)),
                    (kr[:, 3, :], a["ctx_kr"][l]),
                ]
                assert len(loads) == 9
                power(0, 3)
                if l == 0:
                    pool.wait_ge(landed[5], 16)
                for dst, src in loads:
                    pool.dma_start(dst, src).then_inc(layer_in, 16)
                for lo, hi in ((0, 8), (136, 152), (408, 416)):
                    step(nc.gpsimd.memset(upad[:, :, lo:hi], 0.0))
                for t in range(T):
                    power(3 + 8 * t, 8)
                for t in range(T):
                    power(27 + 4 * t, 4)
                pool.wait_ge(layer_in, 16 * 9 * (l + 1))
                for g in range(4):
                    wait_read(pool, l, ("u", g))
                    src, w = upad[:, g, :], 1
                    for k in range(g + 1):
                        dst = win[:, k % 2, :]
                        back, ahead = (1, 0) if k == 0 else (w // 2, w // 2)
                        m = 2 ** g - 2 ** k
                        lo, hi = 8 - m, 408 + m
                        step(nc.gpsimd.tensor_tensor(dst[:, lo:hi], src[:, lo - back:hi - back],
                                                     src[:, lo + ahead:hi + ahead], ALU.add))
                        src, w = dst, 2 * w
                    for p0, t0, n in PSEG:
                        step(nc.gpsimd.tensor_tensor(yaT[:, g, t0:t0 + n], src[:, p0:p0 + n], inv[:, g, t0:t0 + n], ALU.mult))
                    for p0, t0, n in PSEG:
                        nc.gpsimd.tensor_tensor(yaT[:, g, t0:t0 + n], yaT[:, g, t0:t0 + n], upad[:, g, p0:p0 + n],
                                                ALU.subtract).then_inc(pool_ready, 1)
                    pool.wait_ge(pool_ready, 8 * l + 2 * g + 2)
                for t in range(T):
                    power(39 + 8 * t, 8)
                for t in range(4):
                    power(63 + 8 * t, 8)
                wait_full(pool, l, ("o", 7))
                pool.dma_start(gb, a["b_mod"][l, 2 * D:3 * D].partition_broadcast(P)).then_inc(gate_row_in, 16)
                pool.dma_start(g2slot[:, :], a["b_mod"][l, 5 * D:6 * D].partition_broadcast(P)).then_inc(gate_row_in, 16)
                power(95, 3)
                def selection(pr):
                    pool.wait_ge(bank_full[BANK_U[0]], in_pair(l, BANK_U[0], pr, 0) - 1)
                    nc.gpsimd.tensor_copy(gsel, sel[:, :, bass.ds(pr * P, P)]).then_inc(gsel_ready, 1)
                    pool.wait_ge(bank_full[BANK_Y], in_pair(l, BANK_Y, pr, 0) - 3)
                    for e in range(2):
                        nc.gpsimd.tensor_tensor(vsel[:, :, e * SLOTS:(e + 1) * SLOTS],
                                                sel[:, :, bass.ds(pr * P + e * SLOTS, SLOTS)],
                                                aff[:, :, bass.ds(2 * pr + e, 1)].to_broadcast([P, T, SLOTS]), ALU.mult)\
                            .then_inc(vsel_ready, 1)
                pool.wait_ge(sel_ready, 6 * l + 3)
                selection(0)
                pool.wait_ge(sel_ready, 6 * l + 6)
                with pool.Fori(1, NP) as pr:
                    selection(pr)

        @block.scalar
        def _(act):
            step = steps(act, act_step)
            F = nc.scalar.activation
            act.wait_ge(const_in, 48)
            F(cs[:, :, :], cond, ACT.Tanh, scale=0.5).then_inc(cond_tanh, 1)
            sq = [0]

            def square(src, c0, n, more):
                b = sq[0] % 2
                if sq[0] >= 2:
                    act.wait_ge(sq_used, sq[0] - 1)
                dst = sqb[:, b, c0:c0 + n]
                if len(src.shape) == 3:
                    dst = dst.rearrange("p (h d) -> p h d", d=src.shape[2])
                ins = F(dst, src, ACT.Square)
                if more:
                    step(ins)
                else:
                    ins.then_inc(sq_ready, 1)
                    sq[0] += 1

            def x_stats(l, c0):
                for t in range(T):
                    if xs[0]:
                        act.wait_ge(xss_ready, xs[0])
                    F(junk, x[:, t, :], ACT.Square, accum_out=ss[:, c0 + t:c0 + t + 1]).then_inc(xss_ready, 1)
                    xs[0] += 1
            xs = [0]

            def mod_row(l, i):
                ps = wait_full(act, l, ("mod", i))
                read(l, ("mod", i), F(row_of(i), ps[:, :], ACT.Copy))

            def h_evac(l, name, kb):
                k = 0 if name == "h1" else 1
                ps = wait_full(act, l, (name, kb))
                step(F(hT[:, kb, 0:P], ps[:, 0:P], ACT.Identity, scale=amp[k][:, kb, 0:1], bias=shift[k][:, kb, 0:1]))
                read(l, (name, kb), F(hT[:, kb, P:TOK], ps[:, P:TOK], ACT.Identity, scale=amp[k][:, kb, 1:2],
                                      bias=shift[k][:, kb, 1:2]))

            def exps(l, i):
                s = i % 2
                scale = SD ** -0.5 if i < SH else MQ ** -0.5
                act.wait_ge(negm_ready, 16 * l + i + 1)
                sa, _ = turn(l, ("sa", i))
                sbk, _ = turn(l, ("sb", i))
                step(F(prob[:, s, 0:P], bank[sa][:, 0:P], ACT.Exp, bias=negm[:, s, 0:1], scale=scale,
                       accum_out=rsum[:, s, 0:1]))
                read(l, ("sa", i), F(prob[:, s, P:512], bank[sa][:, P:512], ACT.Exp, bias=negm[:, s, 1:2], scale=scale,
                                     accum_out=rsum[:, s, 1:2]))
                if i < SH:
                    F(esink[:, s, :], negm[:, s, :], ACT.Exp, bias=rows[:, ROW_SINK + i:ROW_SINK + i + 1])\
                        .then_inc(sink_ready, 1)
                read(l, ("sb", i), F(prob[:, s, 512:896], bank[sbk][:, 0:TOK], ACT.Exp, bias=negm[:, s, 2:3],
                                     scale=scale, accum_out=rsum[:, s, 2:3]))

            def gate_tanh(l, b, j):
                ps = wait_full(act, l, ("gate", b, j))
                if 8 * b + j >= 2:
                    act.wait_ge(merged_ready, 24 * l + 8 * b + j - 1)
                read(l, ("gate", b, j), F(tanh_g[:, j % 2, :], ps[:, 0:TOK], ACT.Tanh, scale=0.5))

            for l in range(L):
                if l == 0:
                    act.wait_ge(x_in, 32)
                else:
                    x_final(act, l - 1)
                x_stats(l, 0)
                for i in range(4):
                    mod_row(l, i)
                act.wait_ge(cols_ready, 2 * l + 1)
                for kb in range(1, KB, 2):
                    h_evac(l, "h1", kb)
                for t in range(T):
                    square(wait_full(act, l, ("seg", 0, t))[:, :], 0, 512, False)
                for t in range(T):
                    ps = wait_full(act, l, ("seg", 1, t))
                    square(ps[:, 0:P], 0, P, False)
                    step(F(vtok[:, t, :], ps[:, P:2 * P], ACT.Copy))
                    F(qctok[:, t, 0:256], ps[:, 256:512], ACT.Copy).then_inc(cseg_read, 1)
                act.wait_ge(layer_in, 16 * 9 * (l + 1))
                for t in range(T):
                    ps = wait_full(act, l, ("seg", 2, t))
                    step(F(qctok[:, t, 256:QR], ps[:, 0:P], ACT.Copy))
                    c0 = 27 + 4 * t
                    act.wait_ge(cseg_read, 3 * l + t + 1)
                    step(F(yaT[:, 0, 0:QR], qctok[:, t, :], ACT.Square, accum_out=ss[:, c0 + 2:c0 + 3]))
                    step(F(yaT[:, 1, 0:KVR], ps[:, P:QR], ACT.Square, accum_out=ss[:, c0 + 3:c0 + 4]))
                    step(F(kr[:, t, :], ps[:, QR:QR + ROPE], ACT.Copy))
                    F(yaT[:, 2, 32 * t:32 * t + ROPE], kr[:, t, :], ACT.Square, accum_out=sskr[:, t:t + 1])\
                        .then_inc(dseg_read, 1)
                F(yaT[:, 3, 0:ROPE], kr[:, 3, :], ACT.Square, accum_out=sskr[:, 3:4]).then_inc(dseg_read, 1)
                for g in range(4):
                    ps = wait_full(act, l, ("u", g))
                    step(F(upad[:, g, 8:8 + P], ps[:, 0:P], ACT.Copy))
                    read(l, ("u", g), F(upad[:, g, 152:408], ps[:, P:TOK], ACT.Copy))
                mod_row(l, 6)
                for dst, src, s in ((outs[2][0, l], ktok[:, 0, :], ktok_ready), (outs[3][0, l], vtok[:, 0, :], None),
                                    (outs[4][0, l], ckvtok[:, 0, :], ckvtok_ready), (outs[5][0, l], kr[:, 0, :], None)):
                    if s is not None:
                        act.wait_ge(s, 3 * l + 1)
                    act.dma_start(dst, src).then_inc(cache_out, 16)
                for t in range(T):
                    ps = wait_full(act, l, ("tq", t))
                    read(l, ("tq", t), F(qT[:, :, t * P:(t + 1) * P], ps[:, :].rearrange("p (b t) -> p b t", t=P), ACT.Copy))
                for t in range(T):
                    ps = wait_full(act, l, ("tkc", t))
                    if l == 0 and t == 0:
                        act.wait_ge(pads_zero, 3)
                    step(F(kTp[0:SD, 0, t * P:(t + 1) * P], ps[0:SD, 0:P], ACT.Copy))
                    step(F(kTp[SD:P, 1, t * P:(t + 1) * P], ps[SD:P, 0:P], ACT.Copy))
                    read(l, ("tkc", t), F(qcT[:, :, t * P:(t + 1) * P], ps[:, P:512].rearrange("p (b t) -> p b t", t=P),
                                          ACT.Copy))
                ps = wait_full(act, l, ("tkv", 0))
                for t in range(2):
                    ins = F(ckvT[:, :, t * P:(t + 1) * P],
                            ps[:, t * 256:(t + 1) * 256].rearrange("p (b t) -> p b t", t=P), ACT.Copy)
                    if t == 0:
                        step(ins)
                    else:
                        read(l, ("tkv", 0), ins)
                ps = wait_full(act, l, ("tkv", 1))
                read(l, ("tkv", 1), F(ckvT[:, :, 2 * P:TOK], ps[:, 0:256].rearrange("p (b t) -> p b t", t=P), ACT.Copy))
                mod_row(l, 7)
                for t in range(T):
                    for h in range(2):
                        ps = wait_full(act, l, ("wq", h, t))
                        square(ps[:, 0:QR], h * QR, QR, h == 0)
                for g in range(4):
                    ps = wait_full(act, l, ("pool", g))
                    read(l, ("pool", g), F(yaT[:, g, :], ps[:, 0:TOK], ACT.Copy, scale=cols[:, l, COL_PS + g:COL_PS + g + 1]))
                for i in (8, 9):
                    mod_row(l, i)
                act.wait_ge(cache_out, 64 * (l + 1))
                for t in range(4):
                    for h in range(2):
                        ps = wait_full(act, l, ("wkv", t, h))
                        square(ps[:, :].rearrange("p (h c) -> p h c", c=P)[:, :, 0:NOPE], h * 256, 256, h == 0)
                        F(vm[:, t, 4 * h:4 * h + 4, :], ps[:, :].rearrange("p (h c) -> p h c", c=P)[:, :, NOPE:P],
                          ACT.Copy).then_inc(v_read, 1)
                    if t < 3:
                        for h in range(2):
                            ps = wait_full(act, l, ("tqm", t, h))
                            read(l, ("tqm", t, h), F(qmT[0:MQ, 4 * h:4 * h + 4, t * P:(t + 1) * P],
                                                     ps[0:MQ, :].rearrange("p (h t) -> p h t", t=P), ACT.Copy))
                for t in range(4):
                    for h in range(2):
                        ps = wait_full(act, l, ("tkm", t, h))
                        read(l, ("tkm", t, h), F(kmT[0:MQ, 4 * h:4 * h + 4, t * P:(t + 1) * P],
                                                 ps[0:MQ, :].rearrange("p (h t) -> p h t", t=P), ACT.Copy))
                exps(l, 0)
                for i in range(SH + MH):
                    if i < 15:
                        exps(l, i + 1)
                    gate_tanh(l, i // 8, i % 8)
                    ps = wait_full(act, l, ("x", i))
                    read(l, ("x", i), F(probT[:, i % 2, 0:4, :], ps[:, :].rearrange("p (b t) -> p b t", t=P), ACT.Copy))
                    if i % 2:
                        ps = wait_full(act, l, ("o", i // 2))
                        y = ybT if i < 8 else yaT
                        j = (i // 2) % 4
                        read(l, ("o", i // 2), F(y[:, j, :], ps[:, 0:TOK], ACT.Copy))
                for i in (4, 5):
                    mod_row(l, i)
                for j in range(KB):
                    gate_tanh(l, 2, j)
                for t in range(T):
                    act.wait_ge(x_mixed, 3 * l + t + 1)
                    act.wait_ge(xss_ready, xs[0])
                    F(junk, x[:, t, :], ACT.Square, accum_out=ss[:, 95 + t:96 + t]).then_inc(xss_ready, 1)
                    xs[0] += 1
                for i in (10, 11):
                    mod_row(l, i)
                for kb in range(1, KB, 2):
                    h_evac(l, "h2", kb)
                ps = wait_full(act, l, ("rpart", 0))
                read(l, ("rpart", 0), F(rpart, ps[:, 0:TOK], ACT.Copy))
                act.wait_ge(exp_in_ready, l + 1)
                F(aff, logit, ACT.Exp).then_inc(exp_ready, 1)
                k = 1

                def gathered(pr):
                    act.wait_ge(bank_full[0], in_pair(l, 0, pr, 0) + 1)
                    for kb in range(4):
                        v = bank[0][:, kb * P:(kb + 1) * P].rearrange("p (e s) -> p e s", s=SLOTS)
                        F(xcur[:, :, kb, 0:CP], v[:, :, 0:CP], ACT.Identity, scale=amp[k][:, kb, 0:1],
                          bias=shift[k][:, kb, 0:1]).then_inc(xcur_ready, 1)
                        F(xcur[:, :, kb, CP:USED], v[:, :, CP:USED], ACT.Identity, scale=amp[k][:, kb, 1:2],
                          bias=shift[k][:, kb, 1:2]).then_inc(xcur_ready if kb < 3 else bank_read[0], 1)

                def pair_step(pr, more):
                    for h in range(2):
                        b = BANK_G[h]
                        act.wait_ge(bank_full[b], in_pair(l, b, pr, PROJECT[b]) + 1)
                        F(th[h], bank[b][:, :], ACT.Tanh, scale=0.5).then_inc(th_ready, 1)
                    for h in range(2):
                        act.wait_ge(bank_full[BANK_T], in_pair(l, BANK_T, pr, h) + 1)
                        F(hidT[:, 4 * h:4 * h + 4, :], bank[BANK_T][:, :].rearrange("p (b t) -> p b t", t=P), ACT.Copy)\
                            .then_inc(bank_read[BANK_T], 1)
                    act.wait_ge(bank_full[BANK_Y], in_pair(l, BANK_Y, pr, 0) + 1)
                    F(selT, bank[BANK_Y][:, 0:TOK], ACT.Copy).then_inc(bank_read[BANK_Y], 1)
                    if more:
                        gathered(pr + 1)
                gathered(0)
                for_pairs(act, pair_step)

        @block.vector
        def _(dve):
            V = nc.vector
            step = steps(dve, dve_step)
            ev = [0]
            sq = [0]

            def variance(c0, n, width, last=True):
                ins = V.tensor_scalar(var[:, c0:c0 + n], ss[:, c0:c0 + n], 1.0 / width, EPS, ALU.mult, ALU.add)
                if last:
                    ins.then_inc(var_ready, 1)
                else:
                    step(ins)

            def wait_rstd():
                ev[0] += 1
                dve.wait_ge(rstd_ready, ev[0])

            def reduce_squares(h, d, c0):
                dve.wait_ge(sq_ready, sq[0] + 1)
                V.reduce_sum(ss[:, c0:c0 + h], sqb[:, sq[0] % 2, 0:h * d].rearrange("p (h d) -> p h d", d=d), axis=AX)\
                    .then_inc(sq_used, 1)
                sq[0] += 1
                dve.wait_ge(sq_used, sq[0])

            def rotate(v, heads, width, table, last):
                q = width // 4
                n = heads * width
                ra = ropea[:, 0:n].rearrange("p (h d) -> p h d", d=width)
                rb = ropeb[:, 0:n].rearrange("p (h d) -> p h d", d=width)
                cos = table[:, 0, :].unsqueeze(1).to_broadcast([P, heads, width])
                step(V.tensor_tensor(ra, v, cos, ALU.mult))
                sin = table[:, 1, :].rearrange("p (x y f) -> p x y f", y=2, f=q)
                for half in range(2):
                    v5 = v.rearrange("p h (x y f) -> p h x y f", y=2, f=q)[:, :, :, 1 - half, :]
                    o5 = rb.rearrange("p h (x y f) -> p h x y f", y=2, f=q)[:, :, :, half, :]
                    s5 = sin[:, :, half, :].unsqueeze(1).to_broadcast([P, heads, 2, q])
                    step(V.tensor_tensor(o5, v5, s5, ALU.mult))
                last(V.tensor_tensor(v, ra, rb, ALU.add))

            def heads_norm(v, src, r0, heads, width):
                step(V.tensor_tensor(v, src, rstd[:, r0:r0 + heads].unsqueeze(2).to_broadcast([P, heads, width]), ALU.mult))

            def normalise(l, c0):
                for t in range(T):
                    V.tensor_scalar(xn[:, t, :], x[:, t, :], rstd[:, c0 + t:c0 + t + 1], None, ALU.mult)\
                        .then_inc(xn_ready, 1)

            def mod_cols(l, k):
                ps = wait_full(dve, l, ("modcol", k))
                v = ps[:, 0:32].rearrange("p (b s) -> p b s", s=2)
                b0, g0 = COL_B + 24 * k, (COL_N1, COL_N2)[k]

                def col(c):
                    return cols[:, l, c:c + KB].unsqueeze(2).to_broadcast([P, KB, 2])
                step(V.tensor_tensor(shift[k][:, :, :], v[:, 0:KB, :], col(b0), ALU.add))
                b, n = turn(l, ("modcol", k))
                V.tensor_tensor(amp[k][:, :, :], v[:, KB:2 * KB, :], col(b0 + KB), ALU.add).then_inc(bank_read[b], 1)
                dve.wait_ge(bank_read[b], n + 1)
                step(V.tensor_scalar(amp[k][:, :, :], amp[k][:, :, :], 1.0, None, ALU.add))
                V.tensor_tensor(amp[k][:, :, :], amp[k][:, :, :], col(g0), ALU.mult).then_inc(cols_ready, 1)
                dve.wait_ge(cols_ready, 2 * l + k + 1)

            def h_evac(l, name, kb):
                k = 0 if name == "h1" else 1
                ps = wait_full(dve, l, (name, kb))
                step(V.tensor_scalar(hT[:, kb, 0:P], ps[:, 0:P], amp[k][:, kb, 0:1], shift[k][:, kb, 0:1], ALU.mult, ALU.add))
                read(l, (name, kb), V.tensor_scalar(hT[:, kb, P:TOK], ps[:, P:TOK], amp[k][:, kb, 1:2], shift[k][:, kb, 1:2],
                                                    ALU.mult, ALU.add))

            def merge(l, b, j):
                ps = wait_full(dve, l, ("br", b, j))
                wait_read(dve, l, ("gate", b, j))
                dst = merged[:, j, :] if b == 0 else gated
                V.scalar_tensor_tensor(dst, tanh_g[:, j % 2, :], 1.0, ps[:, 0:TOK], ALU.add, ALU.mult)\
                    .then_inc(bank_read[turn(l, ("br", b, j))[0]], 1)
                wait_read(dve, l, ("br", b, j))
                if b:
                    V.tensor_tensor(merged[:, j, :], merged[:, j, :], gated, ALU.add).then_inc(merged_ready, 1)
                else:
                    dve.sem_inc(merged_ready, 1)
                dve.wait_ge(merged_ready, 24 * l + 8 * b + j + 1)

            def maxima(l, i):
                s = i % 2
                sa, sbk = wait_full(dve, l, ("sa", i)), wait_full(dve, l, ("sb", i))
                if i < SH:
                    step(V.tensor_tensor(sa[:, 256:TOK], sa[:, 256:TOK], band[:, 0, :], ALU.add))
                    step(V.tensor_tensor(sbk[:, 0:P], sbk[:, 0:P], band[:, 1, :], ALU.add))
                step(V.reduce_max(mx[:, s, 0:1], sa[:, 0:P], axis=AX))
                step(V.reduce_max(mx[:, s, 1:2], sa[:, P:512], axis=AX))
                step(V.reduce_max(mx[:, s, 2:3], sbk[:, 0:TOK], axis=AX))
                if i < SH:
                    ins = V.tensor_scalar(negm[:, s, :], mx[:, s, :], -SD ** -0.5, negsink[:, i:i + 1], ALU.mult, ALU.min)
                else:
                    ins = V.tensor_scalar(negm[:, s, :], mx[:, s, :], -MQ ** -0.5, None, ALU.mult)
                ins.then_inc(negm_ready, 1)

            def divide(l, i):
                s = i % 2
                wait_read(dve, l, ("sb", i))
                den = rsum[:, s, :]
                if i < SH:
                    dve.wait_ge(sink_ready, SH * l + i + 1)
                    step(V.tensor_tensor(esink[:, s, :], esink[:, s, :], rsum[:, s, :], ALU.add))
                    den = esink[:, s, :]
                step(V.reciprocal(rinv[:, s, :], den))
                for n, (lo, hi) in enumerate(((0, P), (P, 512), (512, 896))):
                    V.tensor_scalar(prob[:, s, lo:hi], prob[:, s, lo:hi], rinv[:, s, n:n + 1], None, ALU.mult)\
                        .then_inc(prob_ready, 1)

            dve.wait_ge(cond_tanh, 1)
            step(V.scalar_tensor_tensor(cs[:, :, :], cs[:, :, :], 1.0, cond, ALU.add, ALU.mult))
            V.tensor_scalar(cs[:, :, :], cs[:, :, :], 0.5, None, ALU.mult).then_inc(cond_ready, 1)

            for l in range(L):
                dve.wait_ge(xss_ready, 6 * l + 3)
                variance(0, 3, D)
                wait_rstd()
                normalise(l, 0)
                mod_cols(l, 0)
                for kb in range(0, KB, 2):
                    h_evac(l, "h1", kb)
                dve.wait_ge(layer_in, 16 * 9 * (l + 1))
                step(V.tensor_scalar(negsink[:, :], rows[:, ROW_SINK:NROW], -1.0, None, ALU.mult))

                def row(c, heads, width):
                    return rows[:, c:c + width].unsqueeze(1).to_broadcast([P, heads, width])
                for t in range(T):
                    reduce_squares(SH, SD, 3 + 8 * t)
                    variance(3 + 8 * t, 8, SD)
                for t in range(T):
                    wait_rstd()
                    q = qtok[:, t, :].rearrange("p (h d) -> p h d", d=SD)
                    b, n = turn(l, ("seg", 0, t))
                    V.tensor_tensor(qtok[:, t, :].rearrange("p (b j d) -> p j b d", j=2, d=SD),
                                    bank[b][:, :].rearrange("p (j b d) -> p j b d", j=2, d=SD),
                                    rstd[:, 3 + 8 * t:11 + 8 * t].rearrange("p (j b) -> p j b", j=2).unsqueeze(3)
                                    .to_broadcast([P, 2, 4, SD]), ALU.mult)\
                        .then_inc(bank_read[b], 1)
                    dve.wait_ge(bank_read[b], n + 1)
                    ins = V.tensor_tensor(q, q, row(ROW_QG, SH, SD), ALU.mult)
                    if t == 0:
                        ins.then_inc(qtok_ready, 1)
                    else:
                        step(ins)
                        rotate(q, SH, SD, ropes[:, t - 1, :, :], lambda i: i.then_inc(qtok_ready, 1))
                for t in range(T):
                    c0 = 27 + 4 * t
                    reduce_squares(2, SD, c0)
                    dve.wait_ge(dseg_read, 4 * l + t + 1)
                    variance(c0, 2, SD, False)
                    variance(c0 + 2, 1, QR, False)
                    variance(c0 + 3, 1, KVR)
                for t in range(T):
                    c0 = 27 + 4 * t
                    wait_rstd()
                    k = ktok[:, t, :].rearrange("p (h d) -> p h d", d=SD)
                    b, n = turn(l, ("seg", 1, t))
                    dve.wait_ge(cseg_read, 3 * l + t + 1)
                    V.tensor_tensor(k, bank[b][:, 0:P].rearrange("p (h d) -> p h d", d=SD),
                                    rstd[:, c0:c0 + 2].unsqueeze(2).to_broadcast([P, 2, SD]), ALU.mult)\
                        .then_inc(bank_read[b], 1)
                    dve.wait_ge(bank_read[b], n + 1)
                    ins = V.tensor_tensor(k, k, row(ROW_KG, 2, SD), ALU.mult)
                    if t == 0:
                        ins.then_inc(ktok_ready, 1)
                    else:
                        step(ins)
                        rotate(k, 2, SD, ropes[:, t - 1, :, :], lambda i: i.then_inc(ktok_ready, 1))
                    V.scalar_tensor_tensor(qctok[:, t, :], qctok[:, t, :], rstd[:, c0 + 2:c0 + 3],
                                           rows[:, ROW_QCG:ROW_QCG + QR], ALU.mult, ALU.mult).then_inc(qctok_ready, 1)
                    b, n = turn(l, ("seg", 2, t))
                    V.scalar_tensor_tensor(ckvtok[:, t, :], bank[b][:, P:QR], rstd[:, c0 + 3:c0 + 4],
                                           rows[:, ROW_KVG:ROW_KVG + KVR], ALU.mult, ALU.mult).then_inc(ckvtok_ready, 1)
                    dve.wait_ge(ckvtok_ready, 3 * l + t + 1)
                    dve.sem_inc(bank_read[b], 1)
                dve.wait_ge(dseg_read, 4 * l + 4)
                step(V.tensor_tensor(krg[:, :, :], kr[:, :, :], row(ROW_MKG + NOPE, 4, ROPE), ALU.mult))
                for t in (1, 2):
                    rotate(krg[:, t:t + 1, :], 1, ROPE, ropem[:, t - 1, :, :], step)
                def query_stats(t):
                    reduce_squares(MH, MQ, 39 + 8 * t)
                    variance(39 + 8 * t, 8, MQ)

                def key_stats(t):
                    c0 = 63 + 8 * t
                    reduce_squares(MH, NOPE, c0)
                    step(V.tensor_scalar(ss[:, c0:c0 + 8], ss[:, c0:c0 + 8], sskr[:, t:t + 1], None, ALU.add))
                    variance(c0, 8, MQ)

                def query(t):
                    c0 = 39 + 8 * t
                    wait_rstd()
                    if t == 2:
                        wait_full(dve, l, ("tqm", 0, 1))
                    v = tok[:, t % 2, :].rearrange("p (h d) -> p h d", d=MQ)
                    for h in range(2):
                        b, n = turn(l, ("wq", h, t))
                        V.tensor_tensor(v[:, 4 * h:4 * h + 4, :], bank[b][:, 0:QR].rearrange("p (h d) -> p h d", d=MQ),
                                        rstd[:, c0 + 4 * h:c0 + 4 * h + 4].unsqueeze(2).to_broadcast([P, 4, MQ]),
                                        ALU.mult).then_inc(bank_read[b], 1)
                        dve.wait_ge(bank_read[b], n + 1)
                    ins = V.tensor_tensor(v, v, row(ROW_MQG, MH, MQ), ALU.mult)
                    if t == 0:
                        ins.then_inc(tok_ready, 1)
                    else:
                        step(ins)
                        rotate(v[:, :, NOPE:MQ], MH, ROPE, ropem[:, t - 1, :, :], lambda i: i.then_inc(tok_ready, 1))

                def key(t):
                    c0 = 63 + 8 * t
                    wait_rstd()
                    wait_full(dve, l, [("tqm", 1, 1), ("tqm", 2, 1), ("tkm", 0, 1), ("tkm", 1, 1)][t])
                    v = tok[:, (3 + t) % 2, :].rearrange("p (h d) -> p h d", d=MQ)
                    for h in range(2):
                        b, n = turn(l, ("wkv", t, h))
                        dve.wait_ge(v_read, 8 * l + 2 * t + h + 1)
                        V.tensor_tensor(v[:, 4 * h:4 * h + 4, 0:NOPE],
                                        bank[b][:, :].rearrange("p (h c) -> p h c", c=P)[:, :, 0:NOPE],
                                        rstd[:, c0 + 4 * h:c0 + 4 * h + 4].unsqueeze(2).to_broadcast([P, 4, NOPE]),
                                        ALU.mult).then_inc(bank_read[b], 1)
                        dve.wait_ge(bank_read[b], n + 1)
                    step(V.tensor_tensor(v[:, :, 0:NOPE], v[:, :, 0:NOPE], row(ROW_MKG, MH, NOPE), ALU.mult))
                    V.tensor_tensor(v[:, :, NOPE:MQ], krg[:, t, :].unsqueeze(1).to_broadcast([P, MH, ROPE]),
                                    rstd[:, c0:c0 + 8].unsqueeze(2).to_broadcast([P, MH, ROPE]), ALU.mult)\
                        .then_inc(tok_ready, 1)
                query_stats(0)
                for t in range(T):
                    if t < 2:
                        query_stats(t + 1)
                    else:
                        key_stats(0)
                    query(t)
                for t in range(4):
                    if t < 3:
                        key_stats(t + 1)
                    key(t)
                    if t == 2:
                        mod_cols(l, 1)
                maxima(l, 0)
                for i in range(SH + MH):
                    divide(l, i)
                    if i < 15:
                        maxima(l, i + 1)
                    ps = wait_full(dve, l, ("y", i))
                    read(l, ("y", i), V.tensor_copy(probT[:, i % 2, 4:7, :], ps[:, 0:TOK].rearrange("p (b t) -> p b t", t=P)))
                    merge(l, i // 8, i % 8)
                dve.wait_ge(gate_row_in, 32 * (l + 1))
                for j in range(KB):
                    merge(l, 2, j)
                    if j < 2:
                        i, c = 4 + j, j * 512
                        for v in range(2):
                            ps = wait_full(dve, l, ("modb", i, v))
                            V.tensor_tensor(g1b[:, v, c:c + 512], ps[:, :], gb[:, c:c + 512], ALU.add)\
                                .then_inc(bank_read[turn(l, ("modb", i, v))[0]], 1)
                            wait_read(dve, l, ("modb", i, v))
                    if j == 2:
                        step(V.tensor_scalar(g1b, g1b, 0.5, None, ALU.mult))
                for n in range(2):
                    for t in range(T):
                        ps = wait_full(dve, l, ("wo", n, t))
                        V.tensor_tensor(wtmp[:, t % 2, :], ps[:, :], g1b[:, min(t, 1), n * 512:(n + 1) * 512], ALU.mult)\
                            .then_inc(bank_read[turn(l, ("wo", n, t))[0]], 1)
                        wait_read(dve, l, ("wo", n, t))
                        xs = x[:, t, n * 512:(n + 1) * 512]
                        ins = V.tensor_tensor(xs, xs, wtmp[:, t % 2, :], ALU.add)
                        if n:
                            ins.then_inc(x_mixed, 1)
                        else:
                            step(ins)
                dve.wait_ge(xss_ready, 6 * l + 6)
                variance(95, 3, D)
                wait_rstd()
                normalise(l, 95)
                for i in (10, 11):
                    ps = wait_full(dve, l, ("modb", i, 0))
                    c = (i - 10) * 512
                    V.tensor_tensor(g2slot[:, c:c + 512], ps[:, :], g2slot[:, c:c + 512], ALU.add)\
                        .then_inc(bank_read[turn(l, ("modb", i, 0))[0]], 1)
                for kb in range(0, KB, 2):
                    h_evac(l, "h2", kb)
                ps = wait_full(dve, l, ("route", 0))
                lg = ps[:, 0:T * NE].rearrange("p (t e) -> p t e", e=NE)
                step(V.reduce_max(small[:, 0:3], lg, axis=AX))
                b, n = turn(l, ("route", 0))
                V.tensor_tensor(logit, lg, small[:, 0:3].unsqueeze(2).to_broadcast([P, T, NE]), ALU.subtract)\
                    .then_inc(bank_read[b], 1)
                dve.wait_ge(bank_read[b], n + 1)
                dve.sem_inc(exp_in_ready, 1)
                dve.wait_ge(exp_ready, l + 1)
                step(V.reduce_sum(small[:, 3:6], aff, axis=AX))
                step(V.reciprocal(small[:, 6:9], small[:, 3:6]))
                V.tensor_tensor(aff, aff, small[:, 6:9].unsqueeze(2).to_broadcast([P, T, NE]), ALU.mult)\
                    .then_inc(aff_ready, 1)
                ps = wait_full(dve, l, ("afft", 0))
                b, n = turn(l, ("afft", 0))
                step(V.tensor_copy(affT[0:NE, :], ps[0:NE, 0:TOK]))
                V.tensor_copy(work[0:NE, :], ps[0:NE, 0:TOK]).then_inc(bank_read[b], 1)
                dve.wait_ge(bank_read[b], n + 1)
                for lo, hi, cap in ((0, P, CP), (P, TOK, CS)):
                    for r in range(cap // 8):
                        if r:
                            step(V.match_replace(work[0:NE, lo:hi], top8[0:NE, :], work[0:NE, lo:hi], -1.0))
                        step(V.max(top8[0:NE, :], work[0:NE, lo:hi]))
                    for k, op in enumerate((ALU.is_gt, ALU.is_equal)):
                        ins = V.tensor_scalar(ge[0:NE, k * TOK + lo:k * TOK + hi], affT[0:NE, lo:hi], top8[0:NE, 7:8], None, op)
                        if lo and k:
                            ins.then_inc(ge_ready, 1)
                        else:
                            step(ins)
                ps = wait_full(dve, l, ("get", 0))
                b, n = turn(l, ("get", 0))
                V.tensor_copy(get, ps[:, 0:T * 2 * NE].rearrange("p (t k) -> p t k", k=2 * NE)).then_inc(bank_read[b], 1)
                dve.wait_ge(bank_read[b], n + 1)
                ps = wait_full(dve, l, ("cum", 0))
                cum = ps[:, 0:T * 2 * NE].rearrange("p (t k) -> p t k", k=2 * NE)
                step(V.tensor_tensor(sl1, get[:, :, 0:NE], cum[:, :, 0:NE], ALU.mult))
                b, n = turn(l, ("cum", 0))
                V.tensor_tensor(sl2, get[:, :, NE:2 * NE], cum[:, :, NE:2 * NE], ALU.mult).then_inc(bank_read[b], 1)
                dve.wait_ge(bank_read[b], n + 1)
                step(V.tensor_tensor(sl1, sl1, sl2, ALU.add))
                step(V.tensor_tensor(sl2, get[:, :, 0:NE], get[:, :, NE:2 * NE], ALU.add))
                step(V.scalar_tensor_tensor(sl1, sl2, -BIG, sl1, ALU.mult, ALU.add))
                step(V.tensor_scalar(sl1, sl1, BIG, None, ALU.add))
                for lo, hi in ((0, 2), (2, NE)):
                    for t in range(T):
                        V.tensor_tensor(sel[:, t, lo * SLOTS:hi * SLOTS].rearrange("p (e s) -> p e s", s=SLOTS),
                                        sl1[:, t, lo:hi].unsqueeze(2).to_broadcast([P, hi - lo, SLOTS]),
                                        slotno[:, min(t, 1), :].unsqueeze(1).to_broadcast([P, hi - lo, SLOTS]),
                                        ALU.is_equal).then_inc(sel_ready, 1)
                k = 1

                def gathered(pr):
                    dve.wait_ge(bank_full[1], in_pair(l, 1, pr, 0) + 1)
                    for kb in range(4, KB):
                        v = bank[1][:, (kb - 4) * P:(kb - 3) * P].rearrange("p (e s) -> p e s", s=SLOTS)
                        V.tensor_scalar(xcur[:, :, kb, 0:CP], v[:, :, 0:CP], amp[k][:, kb, 0:1], shift[k][:, kb, 0:1],
                                        ALU.mult, ALU.add).then_inc(xcur_ready, 1)
                        V.tensor_scalar(xcur[:, :, kb, CP:USED], v[:, :, CP:USED], amp[k][:, kb, 1:2],
                                        shift[k][:, kb, 1:2], ALU.mult, ALU.add)\
                            .then_inc(xcur_ready if kb < KB - 1 else bank_read[1], 1)

                def pair_step(pr, more):
                    for h in range(2):
                        n = l * 2 * NP + pr * 2 + h
                        dve.wait_ge(th_ready, n + 1)
                        V.scalar_tensor_tensor(s1, th[h], 1.0, bank[BANK_G[h]][:, :], ALU.add, ALU.mult)\
                            .then_inc(bank_read[BANK_G[h]], 1)
                        dve.wait_ge(bank_read[BANK_G[h]], in_pair(l, BANK_G[h], pr, PROJECT[BANK_G[h]]) + 1)
                        b = BANK_U[h]
                        dve.wait_ge(bank_full[b], in_pair(l, b, pr, PROJECT[b]) + 1)
                        V.scalar_tensor_tensor(hid[:, h, :], s1, 0.5, bank[b][:, :], ALU.mult, ALU.mult)\
                            .then_inc(bank_read[b], 1)
                        dve.wait_ge(bank_read[b], in_pair(l, b, pr, PROJECT[b]) + 1)
                    if more:
                        gathered(pr + 1)
                    for n in range(2):
                        b = BANK_D[n]
                        dve.wait_ge(bank_full[b], in_pair(l, b, pr, 0) + 1)
                        V.tensor_tensor(osb[:, n * 512:(n + 1) * 512], bank[b][:, :], g2slot[:, n * 512:(n + 1) * 512],
                                        ALU.mult).then_inc(bank_read[b], 1)
                    for s in range(6):
                        n, t = s // 3, s % 3
                        b = (BANK_Y, BANK_T)[s % 2]
                        c = in_pair(l, b, pr, s // 2 + (2 if b == BANK_T else 1)) + 1
                        dve.wait_ge(bank_full[b], c)
                        xs = x[:, t, n * 512:(n + 1) * 512]
                        V.tensor_tensor(xs, xs, bank[b][:, :], ALU.add).then_inc(bank_read[b], 1)
                        dve.wait_ge(bank_read[b], c)
                gathered(0)
                for_pairs(dve, pair_step)

        @block.tensor
        def _(pe):
            mm = nc.tensor.matmul
            turn_over = nc.tensor.transpose

            def begin(l, name):
                b, n = turn(l, name)
                if n:
                    pe.wait_ge(bank_read[b], n)
                return bank[b]

            def done(l, name, ins):
                ins.then_inc(bank_full[turn(l, name)[0]], 1)

            def arrived(l, u):
                n = UNIT_AT[u]
                pe.wait_ge(landed[n % RING], 16 * (l * LANDS[n % RING] + n // RING + 1))

            def mod(l, i):
                ps = begin(l, ("mod", i))
                for h in range(2):
                    arrived(l, ("mod", i, h))
                    w = unit_view(("mod", i, h))
                    for q in range(4):
                        ins = mm(ps[32 * q:32 * q + 32, :], cs[:, 4 * h + q, :], w[:, q, :], start=(h == 0), stop=(h == 1))
                    if h == 0:
                        ins.then_inc(first_half_used, 1)
                done(l, ("mod", i), ins)

            def mod_cols(l, k, i, j, last):
                wait_read(pe, l, ("mod", i))
                ps = bank[turn(l, ("modcol", k))[0]]
                for c in range(4):
                    ins = mm(ps[:, 8 * j + 2 * c:8 * j + 2 * c + 2], row_of(i)[:, c * P:(c + 1) * P], pair,
                             start=True, stop=True)
                if last:
                    done(l, ("modcol", k), ins)

            def norm_turn(l, name, k):
                pe.wait_ge(xn_ready, 6 * l + 3 * k + 3)
                for kb in range(KB):
                    ps = begin(l, (name, kb))
                    for t in range(T):
                        ins = turn_over(ps[:, t * P:(t + 1) * P], xn[:, t, kb * P:(kb + 1) * P], ident)
                    done(l, (name, kb), ins)

            def scores(l, i):
                sa, sbk = begin(l, ("sa", i)), begin(l, ("sb", i))
                if i < SH:
                    q, k = qT[:, i % 4, :], kTp[:, i // 4, :]
                else:
                    q, k = qmT[0:MQ, i - SH, :], kmT[0:MQ, i - SH, :]
                mm(sa[:, 0:P], q[:, 0:P], k[:, 0:P], start=True, stop=True)
                done(l, ("sa", i), mm(sa[:, P:512], q[:, P:2 * P], k[:, P:512], start=True, stop=True))
                done(l, ("sb", i), mm(sbk[:, 0:TOK], q[:, 2 * P:TOK], k[:, P:512], start=True, stop=True))

            def gate(l, b, j):
                ps = begin(l, ("gate", b, j))
                for h in range(2):
                    u = ("gate", (b, j // 4), h)
                    arrived(l, u)
                    w = unit_view(u)
                    for q in range(4):
                        ins = mm(ps[:, 0:TOK], w[:, q, (j % 4) * P:(j % 4 + 1) * P], hT[:, 4 * h + q, :],
                                 start=(h == 0 and q == 0), stop=(h == 1 and q == 3))
                    if h == 0 and j % 4 == 3:
                        ins.then_inc(first_half_used, 1)
                done(l, ("gate", b, j), ins)

            def branch(l, b, j):
                ps = begin(l, ("br", b, j))
                u = ("br", (b, j // 4), 0)
                arrived(l, u)
                if b == 1 and j == 0:
                    for i in range(4):
                        wait_read(pe, l, ("o", i))
                if b == 2 and j == 0:
                    for i in range(4, 8):
                        wait_read(pe, l, ("o", i))
                y = (yaT, ybT, yaT)[b]
                w = unit_view(u)
                for q in range(4):
                    ins = mm(ps[:, 0:TOK], w[:, q, (j % 4) * P:(j % 4 + 1) * P], y[:, q, :], start=(q == 0), stop=(q == 3))
                done(l, ("br", b, j), ins)

            def turn_probs(l, i):
                pe.wait_ge(prob_ready, 48 * l + 3 * i + 3)
                s = i % 2
                for name, at in (("x", range(4)), ("y", range(4, 7))):
                    ps = begin(l, (name, i))
                    for k, n in enumerate(at):
                        c = 0 if n == 0 else P + ((n - 1) % 2) * TOK + ((n - 1) // 2) * P
                        ins = turn_over(ps[:, k * P:(k + 1) * P], prob[:, s, c:c + P], ident)
                    done(l, (name, i), ins)

            def values(l, i):
                s = i % 2
                o = begin(l, ("o", i // 2)) if i % 2 == 0 else bank[turn(l, ("o", i // 2))[0]]
                wait_read(pe, l, ("x", i))
                wait_read(pe, l, ("y", i))
                r = SD * (i % 2)

                def v(t):
                    return vtok[:, t, SD * (i // 4):SD * (i // 4) + SD] if i < SH else vm[:, t, i - SH, :]
                mm(o[r:r + SD, 0:P], v(0), probT[:, s, 0, :], start=True, stop=True)
                for t in range(3):
                    ins = mm(o[r:r + SD, P:TOK], v(1 + t), probT[:, s, 1 + 2 * t:3 + 2 * t, :].rearrange("p a b -> p (a b)"),
                             start=(t == 0), stop=(t == 2))
                if i % 2:
                    done(l, ("o", i // 2), ins)

            pe.wait_ge(const_in, 48)
            pe.wait_ge(cond_ready, 1)
            for l in range(L):
                begin(l, ("modcol", 0))
                mod(l, 0)
                for i in range(1, 4):
                    mod(l, i)
                    mod_cols(l, 0, i - 1, i - 1, False)
                mod_cols(l, 0, 3, 3, True)
                norm_turn(l, "h1", 0)
                for kb in range(KB):
                    wait_read(pe, l, ("h1", kb))
                for s in range(3):
                    n = (512, 512, 416)[s]
                    for h in range(2):
                        arrived(l, ("seg", s, h))
                        w = unit_view(("seg", s, h))
                        for t in range(T):
                            ps = begin(l, ("seg", s, t)) if h == 0 else bank[turn(l, ("seg", s, t))[0]]
                            for q in range(4):
                                ins = mm(ps[:, 0:n], hT[:, 4 * h + q, t * P:(t + 1) * P], w[:, q, 0:n],
                                         start=(h == 0 and q == 0), stop=(h == 1 and q == 3))
                            if h == 0 and t == 2:
                                ins.then_inc(first_half_used, 1)
                            if h == 1:
                                done(l, ("seg", s, t), ins)
                for g in range(4):
                    ps = begin(l, ("u", g))
                    for h in range(2):
                        arrived(l, ("seg", 3, h))
                        w = unit_view(("seg", 3, h))
                        for q in range(4):
                            ins = mm(ps[:, 0:TOK], w[:, q, g * P:(g + 1) * P], hT[:, 4 * h + q, :],
                                     start=(h == 0 and q == 0), stop=(h == 1 and q == 3))
                        if h == 0 and g == 3:
                            ins.then_inc(first_half_used, 1)
                    done(l, ("u", g), ins)
                mod(l, 6)
                for t in range(T):
                    ps = begin(l, ("tq", t))
                    pe.wait_ge(qtok_ready, 3 * l + t + 1)
                    for b in range(4):
                        ins = turn_over(ps[:, b * P:(b + 1) * P], qtok[:, t, b * P:(b + 1) * P], ident)
                    done(l, ("tq", t), ins)
                for t in range(T):
                    ps = begin(l, ("tkc", t))
                    pe.wait_ge(ktok_ready, 3 * l + t + 1)
                    turn_over(ps[:, 0:P], ktok[:, t, :], ident)
                    pe.wait_ge(qctok_ready, 3 * l + t + 1)
                    for b in range(3):
                        ins = turn_over(ps[:, (1 + b) * P:(2 + b) * P], qctok[:, t, b * P:(b + 1) * P], ident)
                    done(l, ("tkc", t), ins)
                for k, tiles in enumerate(((0, 1), (2,))):
                    ps = begin(l, ("tkv", k))
                    for n, t in enumerate(tiles):
                        pe.wait_ge(ckvtok_ready, 3 * l + t + 1)
                        for b in range(2):
                            ins = turn_over(ps[:, (2 * n + b) * P:(2 * n + b + 1) * P], ckvtok[:, t, b * P:(b + 1) * P], ident)
                    done(l, ("tkv", k), ins)
                mod(l, 7)
                for t in range(T):
                    wait_read(pe, l, ("tkc", t))
                for h in range(2):
                    arrived(l, ("wq", h, 0))
                    w = ring[:, slot_of(("wq", h, 0)), 0:3 * QR].rearrange("p (k n) -> p k n", n=QR)
                    for t in range(T):
                        ps = begin(l, ("wq", h, t))
                        for k in range(3):
                            ins = mm(ps[:, 0:QR], qcT[:, k, t * P:(t + 1) * P], w[:, k, :], start=(k == 0), stop=(k == 2))
                        done(l, ("wq", h, t), ins)
                for g in range(4):
                    ps = begin(l, ("pool", g))
                    pe.wait_ge(pool_ready, 8 * l + 2 * g + 2)
                    done(l, ("pool", g), mm(ps[:, 0:TOK], poolw[:, g, :], yaT[:, g, :], start=True, stop=True))
                for i in (8, 9):
                    mod(l, i)
                for k in range(2):
                    wait_read(pe, l, ("tkv", k))
                arrived(l, ("wkv", 0, 0))
                w = ring[:, slot_of(("wkv", 0, 0)), :].rearrange("p (k n) -> p k n", n=D)

                def turn_heads(name, t, n):
                    pe.wait_ge(tok_ready, 7 * l + n + 1)
                    v = tok[:, n % 2, :].rearrange("p (h d) -> p h d", d=MQ)
                    for h in range(2):
                        ps = begin(l, (name, t, h))
                        for k in range(4):
                            ins = turn_over(ps[0:MQ, k * P:(k + 1) * P], v[:, 4 * h + k, :], ident)
                        done(l, (name, t, h), ins)
                for t in range(4):
                    for h in range(2):
                        ps = begin(l, ("wkv", t, h))
                        for k in range(2):
                            ins = mm(ps[:, :], ckvT[:, k, t * P:(t + 1) * P], w[:, k, h * 512:(h + 1) * 512],
                                     start=(k == 0), stop=(k == 1))
                        done(l, ("wkv", t, h), ins)
                    if t < 3:
                        turn_heads("tqm", t, t)
                begin(l, ("modcol", 1))
                for i in range(6, 10):
                    mod_cols(l, 1, i, i - 6, i == 9)
                for t in range(4):
                    turn_heads("tkm", t, 3 + t)
                for t in range(T):
                    wait_read(pe, l, ("tq", t))
                scores(l, 0)
                for g in range(4):
                    wait_read(pe, l, ("pool", g))
                for i in range(SH + MH):
                    if i == 7:
                        for t in range(3):
                            for h in range(2):
                                wait_read(pe, l, ("tqm", t, h))
                        for t in range(4):
                            for h in range(2):
                                wait_read(pe, l, ("tkm", t, h))
                    if i < 15:
                        scores(l, i + 1)
                    gate(l, i // 8, i % 8)
                    turn_probs(l, i)
                    branch(l, i // 8, i % 8)
                    values(l, i)
                for i in (4, 5):
                    mod(l, i)
                for j in range(KB):
                    gate(l, 2, j)
                    branch(l, 2, j)
                    if j < 2:
                        wait_read(pe, l, ("mod", 4 + j))
                        for v in range(2):
                            ps = begin(l, ("modb", 4 + j, v))
                            done(l, ("modb", 4 + j, v), mm(ps[:, :], pick[v], modrow[:, j, :], start=True, stop=True))
                pe.wait_ge(merged_ready, 24 * (l + 1))
                for n in range(2):
                    for h in range(2):
                        arrived(l, ("wo", n, h))
                        w = unit_view(("wo", n, h))
                        for t in range(T):
                            ps = begin(l, ("wo", n, t)) if h == 0 else bank[turn(l, ("wo", n, t))[0]]
                            for q in range(4):
                                ins = mm(ps[:, :], merged[:, 4 * h + q, t * P:(t + 1) * P], w[:, q, :],
                                         start=(h == 0 and q == 0), stop=(h == 1 and q == 3))
                            if h == 0 and t == 2:
                                ins.then_inc(first_half_used, 1)
                            if h == 1:
                                done(l, ("wo", n, t), ins)
                for i in (10, 11):
                    mod(l, i)
                for i in (10, 11):
                    wait_read(pe, l, ("mod", i))
                    ps = begin(l, ("modb", i, 0))
                    done(l, ("modb", i, 0), mm(ps[:, :], pickslot, modrow[:, i % 2, :], start=True, stop=True))
                norm_turn(l, "h2", 1)
                pe.wait_ge(layer_in, 16 * 9 * (l + 1))
                ps = begin(l, ("rpart", 0))
                for kb in range(KB):
                    wait_read(pe, l, ("h2", kb))
                    c = 32 * (kb % 4)
                    ins = mm(ps[c:c + 32, 0:TOK], wrout[:, kb, :], hT[:, kb, :], start=(kb < 4), stop=(kb >= 4))
                done(l, ("rpart", 0), ins)
                wait_read(pe, l, ("rpart", 0))
                ps = begin(l, ("route", 0))
                for t in range(T):
                    ins = mm(ps[:, t * NE:(t + 1) * NE], rpart[:, t * P:(t + 1) * P], fold, start=True, stop=True)
                done(l, ("route", 0), ins)
                ps = begin(l, ("afft", 0))
                pe.wait_ge(aff_ready, l + 1)
                for t in range(T):
                    ins = turn_over(ps[0:NE, t * P:(t + 1) * P], aff[:, t, :], ident)
                done(l, ("afft", 0), ins)
                ps = begin(l, ("get", 0))
                pe.wait_ge(ge_ready, l + 1)
                for t in range(T):
                    for k in range(2):
                        ins = turn_over(ps[:, (2 * t + k) * NE:(2 * t + k + 1) * NE],
                                        ge[0:NE, k * TOK + t * P:k * TOK + (t + 1) * P], ident[0:NE, 0:NE])
                done(l, ("get", 0), ins)
                wait_read(pe, l, ("get", 0))
                ps = begin(l, ("cum", 0))
                for t, before, all_ in ((0, (), (0,)), (1, (), (1, 2)), (2, (1,), (1, 2))):
                    c = 2 * NE * t
                    mm(ps[:, c:c + 2 * NE], tri, get[:, t, :], start=True, stop=False)
                    for k in before:
                        mm(ps[:, c:c + 2 * NE], ones, get[:, k, :], start=False, stop=False)
                    for k in all_:
                        ins = mm(ps[:, c + NE:c + 2 * NE], ones, get[:, k, 0:NE], start=False, stop=(k == all_[-1]))
                done(l, ("cum", 0), ins)

                def gather(pr):
                    pe.wait_ge(gsel_ready, l * NP + pr + 1)
                    for b in range(2):
                        pe.wait_ge(bank_read[b], in_pair(l, b, pr, 0))
                        for kb in range(4 * b, 4 * b + 4):
                            v = bank[b][:, (kb % 4) * P:(kb % 4 + 1) * P].rearrange("p (e s) -> p e s", s=SLOTS)

                            def chosen(t, lo, hi):
                                return gsel[:, t, :].rearrange("p (e s) -> p e s", s=SLOTS)[:, :, lo:hi]
                            mm(v[:, :, 0:CP], xn[:, 0, kb * P:(kb + 1) * P], chosen(0, 0, CP), start=True, stop=True)
                            for t in (1, 2):
                                ins = mm(v[:, :, CP:USED], xn[:, t, kb * P:(kb + 1) * P], chosen(t, CP, USED),
                                         start=(t == 1), stop=(t == 2))
                        ins.then_inc(bank_full[b], 1)

                def pair_step(pr, more):
                    def begin_pair(b, k):
                        pe.wait_ge(bank_read[b], in_pair(l, b, pr, k))

                    def project(g, b, lhs):
                        begin_pair(b, PROJECT[b])
                        for h in range(2):
                            for e in range(2):
                                u = 4 * g + 2 * h + e
                                s = u % RINGX
                                pe.wait_ge(landed[s], 16 * (l * LANDS[s] + LANDED[s] + pr * (24 // RINGX) + u // RINGX + 1))
                            for q in range(4):
                                for e in range(2):
                                    w = expert_slot((4 * g + 2 * h + e) % RINGX)
                                    ins = mm(bank[b][64 * e:64 * e + 64, :], lhs(e, 4 * h + q), w[:, q, :],
                                             start=(h == 0 and q == 0), stop=(h == 1 and q == 3))
                                    if h == 0 and q == 3:
                                        ins.then_inc(first_half_used, 1)
                        ins.then_inc(bank_full[b], 1)

                    pe.wait_ge(xcur_ready, (l * NP + pr + 1) * 14)
                    begin_pair(0, 1)
                    begin_pair(1, 1)
                    for h in range(2):
                        project(2 * h, BANK_G[h], lambda e, kb: xcur[:, e, kb, :])
                        project(2 * h + 1, BANK_U[h], lambda e, kb: xcur[:, e, kb, :])
                    for h in range(2):
                        begin_pair(BANK_T, h)
                        b = BANK_U[h]
                        pe.wait_ge(bank_read[b], in_pair(l, b, pr, PROJECT[b]) + 1)
                        for k in range(4):
                            ins = turn_over(bank[BANK_T][:, k * P:(k + 1) * P], hid[:, h, k * P:(k + 1) * P], ident)
                        ins.then_inc(bank_full[BANK_T], 1)
                    begin_pair(BANK_Y, 0)
                    pe.wait_ge(vsel_ready, l * 2 * NP + 2 * pr + 2)
                    for t in range(T):
                        ins = turn_over(bank[BANK_Y][:, t * P:(t + 1) * P], vsel[:, t, :], ident)
                    ins.then_inc(bank_full[BANK_Y], 1)
                    if more:
                        gather(pr + 1)
                    begin_pair(BANK_T, 2)
                    for n in range(2):
                        project(4 + n, BANK_D[n], lambda e, kb: hidT[:, kb, 64 * e:64 * e + 64])
                    for s in range(6):
                        n, t = s // 3, s % 3
                        if t == 0:
                            pe.wait_ge(bank_read[BANK_D[n]], in_pair(l, BANK_D[n], pr, 0) + 1)
                        b = (BANK_Y, BANK_T)[s % 2]
                        begin_pair(b, s // 2 + (2 if b == BANK_T else 1))
                        mm(bank[b][:, :], selT[:, t * P:(t + 1) * P], osb[:, n * 512:(n + 1) * 512],
                           start=True, stop=True).then_inc(bank_full[b], 1)
                gather(0)
                for_pairs(pe, pair_step)


INPUTS = ["x_prompt", "x_sample", "w_mod", "b_mod", "w_in", "pool_w", "w_q_b", "w_kv_b", "w_br_a", "w_br_b", "w_br_c",
          "w_out", "w_router", "w_gate", "w_up", "w_down"]
OUTPUTS = [(1, P, D), (1, 2 * P, D), (1, L, P, P), (1, L, P, P), (1, L, P, KVR), (1, L, P, ROPE)]


def kernel(**inputs):
    import concourse.bacc as _bacc
    from concourse.bass_utils import run_bass_kernel_spmd as _run

    v = {k: np.asarray(a) for k, a in inputs.items()}
    arrays = {n: v[n] for n in INPUTS}

    def columns(a, n):
        return a.reshape(L, n, P).transpose(2, 0, 1)
    arrays["cols"] = np.concatenate([columns(v["b_mod"], 48), columns(v["norm1_g"], KB), columns(v["norm2_g"], KB),
                                     columns(v["pool_scale"], 4)], axis=2)
    arrays["rows"] = np.concatenate([v["swa_q_g"], v["swa_k_g"], v["mla_q_norm_g"], v["mla_kv_norm_g"], v["mla_q_g"],
                                     v["mla_k_g"], v["sink"]], axis=1)
    cond = np.zeros((P, KB, 32), np.float32)
    cond[:, :, 0] = v["c_ctx"].reshape(KB, P).T
    cond[:, :, 1] = v["c"][0].reshape(KB, P).T
    arrays["condT"] = cond
    arrays["ctx_kT"] = v["cache_swa_k"][0].reshape(L, P, P).transpose(0, 2, 1)
    arrays["ctx_v"] = v["cache_swa_v"][0].reshape(L, P, P)
    arrays["ctx_ckvT"] = v["cache_mla_ckv"][0].transpose(0, 2, 1)
    arrays["ctx_kr"] = v["cache_mla_krope"][0]
    arrays["const"] = const_table()
    arrays["counts"] = count_table()

    nc = _bacc.Bacc("TRN2", target_bir_lowering=False, num_devices=1)
    arrays = {n: np.ascontiguousarray(a) for n, a in arrays.items()}
    aps = {n: nc.dram_tensor(f"in_{n}", a.shape, F32, kind="ExternalInput").ap() for n, a in arrays.items()}
    outs = [nc.dram_tensor(f"out_{i}", s, F32, kind="ExternalOutput").ap() for i, s in enumerate(OUTPUTS)]
    hybrid_step(nc, aps, outs)
    r = _run(nc, [{f"in_{n}": a for n, a in arrays.items()}], core_ids=[0]).results[0]
    got = [r[f"out_{i}"] for i in range(6)]
    got[2] = got[2].reshape(1, L, P, 2, SD)
    got[3] = got[3].reshape(1, L, P, 2, SD)
    return tuple(got)
```
